# Optimizing a Trainium2 kernel written in Bass

```python
import jax
import jax.numpy as jnp
from jax import lax
import numpy as np

D_MODEL = 1024
BATCH = 1
SEQ = 512
DEPTH = 2

CHUNK = 64
N_EVEN = (DEPTH + 1) // 2
N_ODD = DEPTH // 2
EPS = 1e-6
NEG_INF = -1e30

A_WIDTH = 512
A_GROUPS = 8
CONV_W = 3
B_HEADS = 8
B_KV_HEADS = 2
B_HEAD_DIM = 64
WINDOW = 128
WINDOW_CHUNKS = WINDOW // CHUNK
GMLP_CHUNK = 128
C_WIDTH = 512
C_GROUPS = 8
MLA_HEADS = 8
Q_LORA = 384
KV_LORA = 256
NOPE_DIM = 64
ROPE_DIM = 32
V_DIM = 64
ROPE_THETA = 10000.0
Q_BLOCK = 128
FF_HIDDEN = -(-(8 * D_MODEL) // (3 * 256)) * 256

E_IN = 3 * A_WIDTH + (B_HEADS + 2 * B_KV_HEADS) * B_HEAD_DIM
E_MIX = A_WIDTH + B_HEADS * B_HEAD_DIM
E_SPLITS = [A_WIDTH, 2 * A_WIDTH, 3 * A_WIDTH,
            3 * A_WIDTH + B_HEADS * B_HEAD_DIM,
            3 * A_WIDTH + (B_HEADS + B_KV_HEADS) * B_HEAD_DIM]
O_IN = 2 * C_WIDTH + Q_LORA + KV_LORA + ROPE_DIM
O_MIX = C_WIDTH + MLA_HEADS * V_DIM
O_SPLITS = [C_WIDTH, 2 * C_WIDTH, 2 * C_WIDTH + Q_LORA, 2 * C_WIDTH + Q_LORA + KV_LORA]

kernel_name = 'hybrid_chunk_causal_conv_swa_gmlp_mla'

def rmsnorm(x, g):
    xf = x.astype(jnp.float32)
    y = xf * lax.rsqrt(jnp.mean(xf * xf, axis=-1, keepdims=True) + EPS)
    return (y * g.astype(jnp.float32)).astype(x.dtype)

def alibi_slopes(n):
    return 2.0 ** (-8.0 * jnp.arange(1, n + 1, dtype=jnp.float32) / n)

def apply_rope(x, cos, sin):
    half = x.shape[-1] // 2
    x1, x2 = x[..., :half], x[..., half:]
    return jnp.concatenate([x1 * cos - x2 * sin, x2 * cos + x1 * sin], axis=-1)

def short_gated_conv(a_in, a_b, a_c, w):
    s = a_in.shape[1]
    h = a_c * a_in
    hp = jnp.pad(h, ((0, 0), (CONV_W - 1, 0), (0, 0)))
    y = w[0] * hp[:, 0:s]
    for tap in range(1, CONV_W):
        y = y + w[tap] * hp[:, tap:tap + s]
    return a_b * y

def _shift_chunks(t, o):
    return jnp.pad(t, ((0, 0), (o, 0), (0, 0), (0, 0), (0, 0)))[:, :t.shape[1]]

def sliding_window_attention(q, k, v, q_gain, k_gain, sinks):
    b, s = q.shape[:2]
    nc = s // CHUNK
    grp = B_HEADS // B_KV_HEADS
    win = WINDOW_CHUNKS * CHUNK
    q = rmsnorm(q, q_gain)
    k = rmsnorm(k, k_gain)
    qc = q.reshape(b, nc, CHUNK, B_KV_HEADS, grp, B_HEAD_DIM)
    kc = k.reshape(b, nc, CHUNK, B_KV_HEADS, B_HEAD_DIM)
    vc = v.reshape(b, nc, CHUNK, B_KV_HEADS, B_HEAD_DIM)
    offs = range(WINDOW_CHUNKS - 1, -1, -1)
    kb = jnp.concatenate([_shift_chunks(kc, o) for o in offs], axis=2)
    vb = jnp.concatenate([_shift_chunks(vc, o) for o in offs], axis=2)
    scores = jnp.einsum('bcqkgd,bcskd->bckgqs', qc, kb).astype(jnp.float32) * (B_HEAD_DIM ** -0.5)
    qi = jnp.arange(CHUNK)
    kj = jnp.arange(win)
    dist = jnp.abs(qi[:, None] + (WINDOW_CHUNKS - 1) * CHUNK - kj[None, :]).astype(jnp.float32)
    slopes = alibi_slopes(B_HEADS).reshape(B_KV_HEADS, grp)
    scores = scores - slopes[None, None, :, :, None, None] * dist
    key_pos = jnp.arange(nc)[:, None] * CHUNK + kj[None, :] - (WINDOW_CHUNKS - 1) * CHUNK
    scores = jnp.where((key_pos >= 0)[None, :, None, None, None, :], scores, NEG_INF)
    sink = sinks.astype(jnp.float32).reshape(B_KV_HEADS, grp)[None, None, :, :, None, None]
    m = jnp.maximum(jnp.max(scores, axis=-1, keepdims=True), sink)
    p = jnp.exp(scores - m)
    denom = jnp.sum(p, axis=-1, keepdims=True) + jnp.exp(sink - m)
    o = jnp.einsum('bckgqs,bcskd->bcqkgd', (p / denom).astype(v.dtype), vb)
    return o.reshape(b, s, B_HEADS * B_HEAD_DIM)

def spatial_gating(u, v, w_s, bias, v_gain):
    b, s = u.shape[:2]
    n = s // GMLP_CHUNK
    v = rmsnorm(v, v_gain)
    vg = v.reshape(b, n, GMLP_CHUNK, C_GROUPS, C_WIDTH // C_GROUPS)
    pos_chunk = jnp.arange(GMLP_CHUNK) // CHUNK
    mask = pos_chunk[None, :] <= pos_chunk[:, None]
    w = jnp.where(mask[None], w_s, 0.0)
    gate = jnp.einsum('gij,bnjgc->bnigc', w, vg) + bias.T[None, None, :, :, None]
    return u * gate.reshape(b, s, C_WIDTH)

def latent_attention(cq, ckv, kr, q_a_gain, kv_a_gain, w_uq, w_ukv, q_gain, k_gain):
    b, s = cq.shape[:2]
    q = (rmsnorm(cq, q_a_gain) @ w_uq).reshape(b, s, MLA_HEADS, NOPE_DIM + ROPE_DIM)
    kv = (rmsnorm(ckv, kv_a_gain) @ w_ukv).reshape(b, s, MLA_HEADS, NOPE_DIM + V_DIM)
    k_nope, v = kv[..., :NOPE_DIM], kv[..., NOPE_DIM:]
    q_nope = rmsnorm(q[..., :NOPE_DIM], q_gain[:NOPE_DIM])
    q_rope = rmsnorm(q[..., NOPE_DIM:], q_gain[NOPE_DIM:])
    k_nope = rmsnorm(k_nope, k_gain[:NOPE_DIM])
    k_rope = rmsnorm(kr, k_gain[NOPE_DIM:])
    pos = jnp.arange(s, dtype=jnp.float32)
    inv_freq = ROPE_THETA ** (-jnp.arange(0, ROPE_DIM, 2, dtype=jnp.float32) / ROPE_DIM)
    ang = pos[:, None] * inv_freq[None, :]
    cos = jnp.cos(ang).astype(q.dtype)
    sin = jnp.sin(ang).astype(q.dtype)
    q_rope = apply_rope(q_rope, cos[:, None, :], sin[:, None, :])
    k_rope = apply_rope(k_rope, cos, sin)
    qd = NOPE_DIM + ROPE_DIM
    q = jnp.concatenate([q_nope, q_rope], axis=-1) * (qd ** -0.5)
    k = jnp.concatenate([k_nope, jnp.broadcast_to(k_rope[:, :, None, :], (b, s, MLA_HEADS, ROPE_DIM))], axis=-1)
    nqb = s // Q_BLOCK
    qb = q.reshape(b, nqb, Q_BLOCK, MLA_HEADS, qd).transpose(1, 0, 2, 3, 4)
    k_chunk = jnp.arange(s) // CHUNK

    def block(args):
        q_blk, idx = args
        sc = jnp.einsum('bqhd,bkhd->bhqk', q_blk, k).astype(jnp.float32)
        q_chunk = (idx * Q_BLOCK + jnp.arange(Q_BLOCK)) // CHUNK
        sc = jnp.where(k_chunk[None, :] <= q_chunk[:, None], sc, NEG_INF)
        p = jax.nn.softmax(sc, axis=-1).astype(v.dtype)
        return jnp.einsum('bhqk,bkhd->bqhd', p, v)

    o = lax.map(block, (qb, jnp.arange(nqb)))
    return o.transpose(1, 0, 2, 3, 4).reshape(b, s, MLA_HEADS * V_DIM)

def setup_inputs(seed: int = 0) -> dict:
    key = jax.random.key(seed)
    keys = jax.random.split(key, 24)
    counter = [0]

    def nxt():
        k = keys[counter[0]]
        counter[0] += 1
        return k

    def nrm(shape, scale):
        return scale * jax.random.normal(nxt(), shape, jnp.float32)

    def gain(shape):
        return 1.0 + 0.05 * jax.random.normal(nxt(), shape, jnp.float32)

    return {
        'x': nrm((BATCH, SEQ, D_MODEL), 1.0),
        'mix_norm': gain((DEPTH, D_MODEL)),
        'ffn_norm': gain((DEPTH, D_MODEL)),
        'w_ffn_in': nrm((DEPTH, D_MODEL, 2 * FF_HIDDEN), D_MODEL ** -0.5),
        'w_ffn_out': nrm((DEPTH, FF_HIDDEN, D_MODEL), FF_HIDDEN ** -0.5),
        'e_w_in': nrm((N_EVEN, D_MODEL, E_IN), D_MODEL ** -0.5),
        'e_conv': nrm((N_EVEN, CONV_W, A_WIDTH), CONV_W ** -0.5),
        'e_q_gain': gain((N_EVEN, B_HEAD_DIM)),
        'e_k_gain': gain((N_EVEN, B_HEAD_DIM)),
        'e_sinks': nrm((N_EVEN, B_HEADS), 1.0),
        'e_out_gain': gain((N_EVEN, E_MIX)),
        'e_w_out': nrm((N_EVEN, E_MIX, D_MODEL), E_MIX ** -0.5),
        'o_w_in': nrm((N_ODD, D_MODEL, O_IN), D_MODEL ** -0.5),
        'o_spatial': nrm((N_ODD, C_GROUPS, GMLP_CHUNK, GMLP_CHUNK), GMLP_CHUNK ** -0.5),
        'o_spatial_bias': 1.0 + nrm((N_ODD, C_GROUPS, GMLP_CHUNK), 0.1),
        'o_v_gain': gain((N_ODD, C_WIDTH)),
        'o_q_a_gain': gain((N_ODD, Q_LORA)),
        'o_kv_a_gain': gain((N_ODD, KV_LORA)),
        'o_w_uq': nrm((N_ODD, Q_LORA, MLA_HEADS * (NOPE_DIM + ROPE_DIM)), Q_LORA ** -0.5),
        'o_w_ukv': nrm((N_ODD, KV_LORA, MLA_HEADS * (NOPE_DIM + V_DIM)), KV_LORA ** -0.5),
        'o_q_gain': gain((N_ODD, NOPE_DIM + ROPE_DIM)),
        'o_k_gain': gain((N_ODD, NOPE_DIM + ROPE_DIM)),
        'o_out_gain': gain((N_ODD, O_MIX)),
        'o_w_out': nrm((N_ODD, O_MIX, D_MODEL), O_MIX ** -0.5),
    }

def reference(x, mix_norm, ffn_norm, w_ffn_in, w_ffn_out,
              e_w_in, e_conv, e_q_gain, e_k_gain, e_sinks, e_out_gain, e_w_out,
              o_w_in, o_spatial, o_spatial_bias, o_v_gain, o_q_a_gain, o_kv_a_gain,
              o_w_uq, o_w_ukv, o_q_gain, o_k_gain, o_out_gain, o_w_out):
    b, s = x.shape[:2]
    for layer in range(DEPTH):
        h = rmsnorm(x, mix_norm[layer])
        if layer % 2 == 0:
            i = layer // 2
            z = h @ e_w_in[i]
            a_in, a_b, a_c, bq, bk, bv = jnp.split(z, E_SPLITS, axis=-1)
            ya = short_gated_conv(a_in, a_b, a_c, e_conv[i])
            yb = sliding_window_attention(
                bq.reshape(b, s, B_HEADS, B_HEAD_DIM),
                bk.reshape(b, s, B_KV_HEADS, B_HEAD_DIM),
                bv.reshape(b, s, B_KV_HEADS, B_HEAD_DIM),
                e_q_gain[i], e_k_gain[i], e_sinks[i])
            g = e_out_gain[i]
            y = jnp.concatenate([rmsnorm(ya, g[:A_WIDTH]), rmsnorm(yb, g[A_WIDTH:])], axis=-1) @ e_w_out[i]
        else:
            i = layer // 2
            z = h @ o_w_in[i]
            c_u, c_v, cq, ckv, kr = jnp.split(z, O_SPLITS, axis=-1)
            yc = spatial_gating(jax.nn.gelu(c_u), jax.nn.gelu(c_v), o_spatial[i], o_spatial_bias[i], o_v_gain[i])
            yd = latent_attention(cq, ckv, kr, o_q_a_gain[i], o_kv_a_gain[i], o_w_uq[i], o_w_ukv[i],
                                  o_q_gain[i], o_k_gain[i])
            g = o_out_gain[i]
            y = jnp.concatenate([rmsnorm(yc, g[:C_WIDTH]), rmsnorm(yd, g[C_WIDTH:])], axis=-1) @ o_w_out[i]
        x = x + y
        h = rmsnorm(x, ffn_norm[layer])
        gate, up = jnp.split(h @ w_ffn_in[layer], 2, axis=-1)
        x = x + (jax.nn.silu(gate) * up) @ w_ffn_out[layer]
    return x


_drawn_inputs = setup_inputs


def setup_inputs(seed=0):
    import zlib

    import numpy as np

    out = dict(_drawn_inputs(seed))
    spreads = {}
    factors = {'o_v_gain': 4.391, 'o_q_a_gain': 3.913, 'o_q_gain': 3.8, 'o_k_gain': 4.626}
    for name, (base, spread) in spreads.items():
        noise = np.random.default_rng([zlib.crc32(name.encode()), seed]).standard_normal(out[name].shape)
        drawn = base * np.exp(spread * noise) if base else spread * noise
        out[name] = jnp.asarray(drawn.astype(out[name].dtype))
    for name, factor in factors.items():
        out[name] = (out[name] * factor).astype(out[name].dtype)
    return out
```

```python
from contextlib import ExitStack

import numpy as np
import concourse.bass as bass
from concourse import mybir

F32 = mybir.dt.float32
F32R = mybir.dt.float32r
BF16 = mybir.dt.bfloat16

ACT = mybir.ActivationFunctionType
ALU = mybir.AluOpType
AX = mybir.AxisListType.X

P = 128
S = 512
D = 1024
DT = D // P
FF = 2816
FT = FF // P
NG_FF = FF // 256
EPS = 1e-6
HEADS = 8
QT = S // P
E_SCALE = 64 ** -0.5
O_SCALE = 96 ** -0.5
NEG = -1e30

RAW_SLOTS = 2
W_SLOTS = 4
LEAD = W_SLOTS

E_Q, E_KV, E_AIN, E_AC, E_AB, E_OUT = 0, 4, 6, 10, 14, 18
FFN_IN = (26, 122)
FFN_OUT = (70, 166)
O_CQ, O_CKV, O_CV, O_UQ, O_UKV, O_CU, O_OUT = 92, 96, 100, 104, 108, 110, 114
N_LOADS = 188

(M_MIX0, M_EQ, M_EK, M_EB, M_EA, M_FFN0, M_MIX1, M_CQ, M_CKV, M_KR, M_OQ, M_OK, M_OC, M_OD,
 M_FFN1) = (0, 1, 5, 6, 7, 8, 9, 10, 11, 12, 13, 21, 25, 26, 27)
TO_ROW_SCALE = (M_MIX0, M_FFN0, M_MIX1, M_FFN1)

G_FFN0, G_MIX1, G_FFN1, G_EA, G_EB, G_CONV, G_OOUT = 0, 8, 16, 24, 28, 32, 44
G_CQ, G_CKV, G_V, G_EQ, G_EK, G_OQE, G_OQO, G_OK, G_KR, G_KRS = 52, 55, 57, 61, 62, 63, 64, 65, 66, 67
N_GAINS = 68
N_SMALL = 640
TAB_C, TAB_S, TAB_EVEN, TAB_ODD = 0, 512, 1024, 1536


def load_width(n):
    if O_CQ <= n < O_CKV:
        return 768
    if O_UQ <= n < O_UKV:
        return 768
    return 1024


def ordered(n, split, source):
    if E_Q <= n < E_KV:
        if source is not None:
            return [source[:, 512 * k:512 * k + 512].rearrange("p (g j c) -> p g j c", g=2, j=4) for k in range(2)]
        return [split[:, 512 * k:512 * k + 512].rearrange("p (j g c) -> p g j c", g=2, j=4) for k in range(2)]
    if O_UKV <= n < O_CU:
        if source is not None:
            return [source[:, 512 * k:512 * k + 512].rearrange("p (h two c) -> p h two c", h=4, two=2) for k in range(2)]
        return [split[:, 512 * k:512 * k + 512].rearrange("p (two h c) -> p h two c", h=4, two=2) for k in range(2)]
    w = load_width(n)
    return [(split if source is None else source)[:, 0:w]]


def load_dmas(n):
    if E_Q <= n < E_KV:
        return 1
    if n in (E_OUT, E_OUT + 1, E_OUT + 4, E_OUT + 5):
        return 2
    if O_UQ <= n < O_UKV:
        return 3
    return 1


def landed(n):
    return 16 * sum(load_dmas(m) for m in range(n % RAW_SLOTS, n + 1, RAW_SLOTS))


GAIN_DMAS = 10 + 6 + 3 + 4 + 12


def program(nc, x, mix_norm, ffn_norm, w_ffn_in, w_ffn_out, e_w_in, e_conv, e_q_gain, e_k_gain,
            e_sinks, e_out_gain, e_w_out, o_w_in, o_spatial, o_spatial_bias, o_v_gain,
            o_q_a_gain, o_kv_a_gain, o_w_uq, o_w_ukv, o_q_gain, o_k_gain, o_out_gain, o_w_out,
            c_small, c_tables, c_alibi, out):
    ctx = ExitStack()
    base = (nc.sbuf_base + 31) // 32 * 32
    top = nc.sbuf_top
    place = [base]

    def at(name, shape, dt, offset):
        return nc.alloc_sbuf_tensor_at(name, shape, dt, offset=offset)

    def sb(name, shape, dt=F32, size=4):
        n = size
        for d in shape[1:]:
            n *= d
        t = at(name, shape, dt, place[0])
        place[0] += (n + 31) // 32 * 32
        return t

    xT = sb("xT", [P, DT, S])
    h_at = place[0]
    h_hi = sb("h_hi", [P, DT, S], F32R)
    h_lo = sb("h_lo", [P, DT, S], F32R)
    out_tok = at("out_tok", [P, QT, D], F32, h_at)
    raw = sb("raw", [P, RAW_SLOTS, 1024])
    w_hi = sb("w_hi", [P, W_SLOTS, 1024], F32R)
    w_lo = sb("w_lo", [P, W_SLOTS, 1024], F32R)
    small = sb("small", [P, N_SMALL])
    ident, ones = small[:, 0:128], small[:, 128:256]
    mean64, mean_even, mean_odd = small[:, 256:384], small[:, 384:512], small[:, 512:640]
    tables = sb("tables", [P, 2048])
    gains = sb("gains", [P, N_GAINS])
    mix0_gain = sb("mix0_gain", [P, DT])
    gate_bias = sb("gate_bias", [P, 4, P])
    sinks = sb("sinks", [P, HEADS])
    eps_col = sb("eps_col", [P, 1])
    zero_col = sb("zero_col", [P, 1])
    mask_q = sb("mask_q", [1, P], BF16, 2)
    mask_k = sb("mask_k", [1, P], BF16, 2)
    tiny = sb("tiny", [P, 16, 8])
    row_scale = sb("row_scale", [P, S])
    acc = sb("acc", [P, S])
    temp_at = place[0]
    sq = sb("sq", [P, 2, S])
    y0 = sb("y0", [P, 2, S])
    rs = sb("rs", [P, 2, S])
    ffn_t = at("ffn_t", [P, 4, S], F32, temp_at)
    R = place[0]
    K = 1024
    act_hi = at("act_hi", [P, FT, S], F32R, R)
    act_lo = at("act_lo", [P, FT, S], F32R, R + FT * S * 4)
    assert R + 2 * FT * S * 4 <= top, (R + 2 * FT * S * 4, top)
    x_tok = at("x_tok", [P, QT, D], F32, R)
    e_sc = at("e_sc", [P, 2, HEADS, 256], F32, R)
    yb_hi = at("yb_hi", [P, 4, S], F32R, R)
    yb_lo = at("yb_lo", [P, 4, S], F32R, R + 8 * K)
    alibi = at("alibi", [P, HEADS, 256], F32, R + 16 * K)
    e_pT = at("e_pT", [P, 4, S], F32, R + 24 * K)
    e_q = at("e_q", [P, 4, S], F32, R + 32 * K)
    e_k = at("e_k", [P, S], F32, R + 40 * K)
    e_vT = at("e_vT", [P, S], F32, R + 42 * K)
    e_v = at("e_v", [P, QT, P], F32, R + 44 * K)
    conv_h = at("conv_h", [P, 4, S], F32, R + 46 * K)
    conv_y = at("conv_y", [P, 4, S], F32, R + 54 * K)
    yb = at("yb", [P, 4, S], F32, R + 62 * K)
    ya_hi = at("ya_hi", [P, 4, S], F32R, R + 70 * K)
    ya_lo = at("ya_lo", [P, 4, S], F32R, R + 78 * K)
    gain_rows = at("gain_rows", [N_GAINS, P], F32, R + 86 * K)
    o_q = at("o_q", [P, HEADS, S], F32, R)
    yd_hi = at("yd_hi", [P, 4, S], F32R, R)
    yd_lo = at("yd_lo", [P, 4, S], F32R, R + 8 * K)
    o_k = at("o_k", [P, HEADS, S], F32, R + 16 * K)
    o_v = at("o_v", [P, QT, S], F32, R + 32 * K)
    o_p = at("o_p", [P, 2, QT, S], F32, R + 40 * K)
    cq = at("cq", [P, 3, S], F32, R + 40 * K)
    k_pair = at("k_pair", [P, 4, S], F32, R + 40 * K)
    u_c = at("u_c", [P, 4, S], F32, R + 40 * K)
    w_sp = at("w_sp", [P, HEADS, P], F32, R + 48 * K)
    kr = at("kr", [P, 2, S], F32, R + 52 * K)
    yc = at("yc", [P, 4, S], F32, R + 48 * K)
    o_pT = at("o_pT", [P, 3, S], F32, R + 56 * K)
    cq_hi = at("cq_hi", [P, 3, S], F32R, R + 56 * K)
    cq_lo = at("cq_lo", [P, 3, S], F32R, R + 62 * K)
    ckv = at("ckv", [P, 2, S], F32, R + 68 * K)
    w_spT = at("w_spT", [P, HEADS, P], F32, R + 68 * K)
    yd = at("yd", [P, 4, S], F32, R + 64 * K)
    v_c = at("v_c", [P, QT, S], F32, R + 72 * K)
    ckv_hi = at("ckv_hi", [P, 2, S], F32R, R + 80 * K)
    ckv_lo = at("ckv_lo", [P, 2, S], F32R, R + 84 * K)
    yc_hi = at("yc_hi", [P, 4, S], F32R, R + 72 * K)
    yc_lo = at("yc_lo", [P, 4, S], F32R, R + 80 * K)

    ps = ctx.enter_context(nc.psum_tensor("ps", [P, 8, S], F32))

    def sem(name):
        return ctx.enter_context(nc.semaphore(name))

    raw_landed = [sem(f"raw_landed{i}") for i in range(RAW_SLOTS)]
    hi_done = sem("hi_done")
    lo_done = sem("lo_done")
    load_used = sem("load_used")
    small_loaded = sem("small_loaded")
    x_loaded = sem("x_loaded")
    mix0_loaded = sem("mix0_loaded")
    tables_loaded = sem("tables_loaded")
    alibi_loaded = sem("alibi_loaded")
    gain_rows_loaded = sem("gain_rows_loaded")
    sinks_loaded = sem("sinks_loaded")
    gate_bias_loaded = sem("gate_bias_loaded")
    columns_set = sem("columns_set")
    spatial_loaded = sem("spatial_loaded")
    spatial_zeroed = sem("spatial_zeroed")
    x_turned = sem("x_turned")
    x_ready = sem("x_ready")
    h_hi_ready = sem("h_hi_ready")
    h_squared = sem("h_squared")
    h_lo_ready = sem("h_lo_ready")
    h_summed = sem("h_summed")
    gains_turned = sem("gains_turned")
    gains_ready = sem("gains_ready")
    sums_ready = sem("sums_ready")
    rs_first = sem("rs_first")
    rs_square = sem("rs_square")
    rs_step = sem("rs_step")
    rs_ready = sem("rs_ready")
    rs_used = sem("rs_used")
    e_q_scaled = sem("e_q_scaled")
    e_q_squared = sem("e_q_squared")
    e_k_scaled = sem("e_k_scaled")
    e_k_squared = sem("e_k_squared")
    e_v_scaled = sem("e_v_scaled")
    e_v_turned = sem("e_v_turned")
    e_v_ready = sem("e_v_ready")
    conv_in_scaled = sem("conv_in_scaled")
    conv_in_ready = sem("conv_in_ready")
    conv_h_ready = sem("conv_h_ready")
    conv_tap_a = sem("conv_tap_a")
    conv_tap_b = sem("conv_tap_b")
    conv_tap_c = sem("conv_tap_c")
    conv_y_scaled = sem("conv_y_scaled")
    a_scores = sem("a_scores")
    a_biased = sem("a_biased")
    a_row_max = sem("a_row_max")
    a_max = sem("a_max")
    a_neg_max = sem("a_neg_max")
    a_sink_diff = sem("a_sink_diff")
    a_exp_done = sem("a_exp_done")
    a_sink_exp = sem("a_sink_exp")
    a_denominator = sem("a_denominator")
    a_inverse = sem("a_inverse")
    a_probs = sem("a_probs")
    a_probs_turned = sem("a_probs_turned")
    a_pT_act = sem("a_pT_act")
    a_pT_dve = sem("a_pT_dve")
    a_values = sem("a_values")
    a_out = sem("a_out")
    yb_squared = sem("yb_squared")
    yb_summed = sem("yb_summed")
    yb_normed = sem("yb_normed")
    yb_hi_ready = sem("yb_hi_ready")
    yb_lo_ready = sem("yb_lo_ready")
    ya_ready = sem("ya_ready")
    ya_squared = sem("ya_squared")
    ya_summed = sem("ya_summed")
    ya_normed = sem("ya_normed")
    ya_hi_ready = sem("ya_hi_ready")
    ya_lo_ready = sem("ya_lo_ready")
    gate_scaled = sem("gate_scaled")
    silu_done = sem("silu_done")
    silu_scaled = sem("silu_scaled")
    hidden_ready = sem("hidden_ready")
    hidden_hi = sem("hidden_hi")
    hidden_lo = sem("hidden_lo")
    tok_sums = sem("tok_sums")
    tok_first = sem("tok_first")
    tok_square = sem("tok_square")
    tok_step = sem("tok_step")
    tok_scale = sem("tok_scale")
    cq_scaled = sem("cq_scaled")
    cq_squared = sem("cq_squared")
    cq_summed = sem("cq_summed")
    cq_normed = sem("cq_normed")
    cq_hi_ready = sem("cq_hi_ready")
    cq_lo_ready = sem("cq_lo_ready")
    ckv_scaled = sem("ckv_scaled")
    ckv_squared = sem("ckv_squared")
    ckv_summed = sem("ckv_summed")
    ckv_normed = sem("ckv_normed")
    ckv_hi_ready = sem("ckv_hi_ready")
    ckv_lo_ready = sem("ckv_lo_ready")
    kr_normed = sem("kr_normed")
    kr_turning = sem("kr_turning")
    kr_rotated = sem("kr_rotated")
    kr_copied = sem("kr_copied")
    kr_columns = sem("kr_columns")
    uq_columns = sem("uq_columns")
    spatial_turned = sem("spatial_turned")
    spatial_ready = sem("spatial_ready")
    cv_ready = sem("cv_ready")
    cv_squared = sem("cv_squared")
    cv_first = sem("cv_first")
    cv_square = sem("cv_square")
    cv_step = sem("cv_step")
    cv_scale = sem("cv_scale")
    cv_normed = sem("cv_normed")
    oq_squared = sem("oq_squared")
    oq_turned = sem("oq_turned")
    ok_squared = sem("ok_squared")
    ok_gained = sem("ok_gained")
    ok_normed = sem("ok_normed")
    ov_act = sem("ov_act")
    ov_dve = sem("ov_dve")
    gates_mixed = sem("gates_mixed")
    gates_ready = sem("gates_ready")
    u_scaled = sem("u_scaled")
    u_ready = sem("u_ready")
    yc_ready = sem("yc_ready")
    yc_squared = sem("yc_squared")
    yc_summed = sem("yc_summed")
    yc_normed = sem("yc_normed")
    yc_hi_ready = sem("yc_hi_ready")
    yc_lo_ready = sem("yc_lo_ready")
    d_scores = sem("d_scores")
    d_max = sem("d_max")
    d_neg_max = sem("d_neg_max")
    d_exp_done = sem("d_exp_done")
    d_inverse = sem("d_inverse")
    d_probs = sem("d_probs")
    d_probs_turned = sem("d_probs_turned")
    d_pT_act = sem("d_pT_act")
    d_pT_dve = sem("d_pT_dve")
    d_values = sem("d_values")
    d_out = sem("d_out")
    yd_squared = sem("yd_squared")
    yd_summed = sem("yd_summed")
    yd_normed = sem("yd_normed")
    yd_hi_ready = sem("yd_hi_ready")
    yd_lo_ready = sem("yd_lo_ready")
    out_turned = sem("out_turned")
    out_act = sem("out_act")
    out_dve = sem("out_dve")
    out_stored = sem("out_stored")

    block = ctx.enter_context(nc.Block())

    @block.sync
    def _(sp):
        sp.dma_start(small[:, :], c_small).then_inc(small_loaded, 16)
        for t in range(QT):
            sp.dma_start(x_tok[:, t, :], x[0, t * P:(t + 1) * P, :]).then_inc(x_loaded, 16)

        def free(n):
            if n >= RAW_SLOTS:
                sp.wait_ge(lo_done, n - RAW_SLOTS + 1)

        def wide(n, w, rows, c0, cols):
            free(n)
            dst = raw[:, n % 2, 0:2 * cols].rearrange("p (k n) -> p k n", k=2)
            src = w[rows:rows + 256, c0:c0 + cols].rearrange("(k p) n -> p k n", p=P)
            sp.dma_start(dst, src).then_inc(raw_landed[n % 2], 16)

        ein = e_w_in[0]
        for j in range(4):
            wide(E_Q + j, ein, 256 * j, 1536, 512)
        for j in range(2):
            n = E_KV + j
            free(n)
            sp.dma_start(raw[:, n % 2, :].rearrange("p (k n) -> p k n", k=4),
                         ein[512 * j:512 * j + 512, 2048:2304].rearrange("(k p) n -> p k n", p=P)
                         ).then_inc(raw_landed[n % 2], 16)
        for s0, c0 in ((E_AIN, 0), (E_AC, 1024), (E_AB, 512)):
            for j in range(4):
                wide(s0 + j, ein, 256 * j, c0, 512)
        for half in range(2):
            for j in range(2):
                n = E_OUT + 4 * half + j
                free(n)
                for g in range(2):
                    r0 = 512 + 256 * g + 128 * j
                    sp.dma_start(raw[64 * g:64 * g + 64, n % 2, :].rearrange("p (k n) -> p k n", k=2),
                                 e_w_out[0, r0:r0 + 128, 512 * half:512 * half + 512]
                                 .rearrange("(k p) n -> p k n", p=64)).then_inc(raw_landed[n % 2], 16)
            for j in range(2):
                wide(E_OUT + 4 * half + 2 + j, e_w_out[0], 256 * j, 512 * half, 512)

        def ffn(layer):
            n0 = FFN_IN[layer]
            w = w_ffn_in[layer].rearrange("(k p) n -> p k n", p=P)
            with sp.Fori(0, NG_FF) as g:
                for j in range(4):
                    kh, two = j // 2, j % 2
                    sp.wait_ge(lo_done, n0 + j - 1 + 4 * g)
                    sp.dma_start(raw[:, (n0 + j) % 2, :].rearrange("p (k n) -> p k n", k=4),
                                 w[:, 4 * kh:4 * kh + 4, bass.ds(FF * two + g * 256, 256)]
                                 ).then_inc(raw_landed[(n0 + j) % 2], 16)
            n1 = FFN_OUT[layer]
            w = w_ffn_out[layer].rearrange("(k p) n -> p k n", p=P)
            for half in range(2):
                with sp.Fori(0, 5) as i:
                    for j in range(2):
                        n = n1 + 11 * half + j
                        sp.wait_ge(lo_done, n - 1 + 2 * i)
                        sp.dma_start(raw[:, n % 2, :].rearrange("p (k n) -> p k n", k=2),
                                     w[:, bass.ds(4 * i + 2 * j, 2), 512 * half:512 * half + 512]
                                     ).then_inc(raw_landed[n % 2], 16)
                wide(n1 + 11 * half + 10, w_ffn_out[layer], 20 * P, 512 * half, 512)

        ffn(0)
        oin = o_w_in[0]
        for j in range(4):
            wide(O_CQ + j, oin, 256 * j, 1024, 384)
        for j in range(4):
            n = O_CKV + j
            free(n)
            sp.dma_start(raw[:, n % 2, :].rearrange("p (k n) -> p k n", k=2)[:, :, 0:288],
                         oin[256 * j:256 * j + 256, 1408:1696].rearrange("(k p) n -> p k n", p=P)
                         ).then_inc(raw_landed[n % 2], 16)
        sp.wait_ge(load_used, FFN_OUT[0] + 22)
        sp.wait_ge(spatial_zeroed, 1)
        ws = o_spatial[0].rearrange("g i j -> i g j")
        sp.dma_start(w_sp[0:64, :, 0:64], ws[0:64, :, 0:64]).then_inc(spatial_loaded, 16)
        sp.dma_start(w_sp[64:128, :, :], ws[64:128, :, :]).then_inc(spatial_loaded, 16)
        for j in range(4):
            wide(O_CV + j, oin, 256 * j, 512, 512)
        for j in range(4):
            n = O_UQ + j
            free(n)
            dst = raw[:, n % 2, 0:768].rearrange("p (k n) -> p k n", k=3)
            src = o_w_uq[0].rearrange("(k p) n -> p k n", p=P)
            he, ho = 96 * 2 * j, 96 * (2 * j + 1)
            sp.dma_start(dst[:, :, 0:96], src[:, :, he:he + 96]).then_inc(raw_landed[n % 2], 16)
            sp.dma_start(dst[:, :, 128:160], src[:, :, ho + 64:ho + 96]).then_inc(raw_landed[n % 2], 16)
            sp.dma_start(dst[:, :, 192:256], src[:, :, ho:ho + 64]).then_inc(raw_landed[n % 2], 16)
        for j in range(2):
            wide(O_UKV + j, o_w_ukv[0], 0, 512 * j, 512)
        for j in range(4):
            wide(O_CU + j, oin, 256 * j, 0, 512)
        for half in range(2):
            for j in range(4):
                wide(O_OUT + 4 * half + j, o_w_out[0], 256 * j, 512 * half, 512)
        ffn(1)
        for half in range(2):
            sp.wait_ge(out_act, 2 * half + 2)
            sp.wait_ge(out_dve, 2 * half + 2)
            for t in range(QT):
                sp.dma_start(out[0, t * P:(t + 1) * P, 512 * half:512 * half + 512],
                             out_tok[:, t, 512 * half:512 * half + 512]).then_inc(out_stored, 16)
        sp.wait_ge(out_stored, 16 * 8)

    @block.gpsimd
    def _(pool):
        rows = gain_rows
        pool.memset(eps_col[:, :], EPS)
        pool.memset(zero_col[:, :], 0.0)
        pool.memset(mask_q[:, 0:64], 1.0)
        pool.memset(mask_q[:, 64:128], 0.0)
        pool.memset(mask_k[:, 0:64], 0.0)
        pool.memset(mask_k[:, 64:128], NEG).then_inc(columns_set, 1)
        n_gain = [0]

        def row(dst, src):
            pool.dma_start(dst, src).then_inc(gain_rows_loaded, 16)
            n_gain[0] += 1

        row(rows[G_FFN0:G_FFN0 + 8, :], ffn_norm[0].rearrange("(r c) -> r c", c=P))
        row(rows[G_MIX1:G_MIX1 + 8, :], mix_norm[1].rearrange("(r c) -> r c", c=P))
        row(rows[G_FFN1:G_FFN1 + 8, :], ffn_norm[1].rearrange("(r c) -> r c", c=P))
        row(rows[G_EA:G_EA + 4, :], e_out_gain[0, 0:512].rearrange("(r c) -> r c", c=P))
        row(rows[G_EB:G_EB + 4, :].rearrange("r (g c) -> r g c", g=2),
            e_out_gain[0, 512:1024].rearrange("(g r c) -> r g c", g=2, c=64))
        row(rows[G_CONV:G_CONV + 12, :], e_conv[0].rearrange("t (r c) -> (t r) c", c=P))
        row(rows[G_OOUT:G_OOUT + 8, :], o_out_gain[0].rearrange("(r c) -> r c", c=P))
        row(rows[G_CQ:G_CQ + 3, :], o_q_a_gain[0].rearrange("(r c) -> r c", c=P))
        row(rows[G_CKV:G_CKV + 2, :], o_kv_a_gain[0].rearrange("(r c) -> r c", c=P))
        row(rows[G_V:G_V + 4, :], o_v_gain[0].rearrange("(r c) -> r c", c=P))
        for r, g in ((G_EQ, e_q_gain), (G_EK, e_k_gain), (G_OK, o_k_gain)):
            for i in range(2):
                row(rows[r:r + 1, 64 * i:64 * i + 64], g[0:1, 0:64])
        row(rows[G_OQE:G_OQE + 1, 0:96], o_q_gain[0:1, 0:96])
        row(rows[G_OQE:G_OQE + 1, 96:112], o_q_gain[0:1, 80:96])
        row(rows[G_OQE:G_OQE + 1, 112:128], o_q_gain[0:1, 64:80])
        row(rows[G_OQO:G_OQO + 1, 0:32], o_q_gain[0:1, 64:96])
        row(rows[G_OQO:G_OQO + 1, 32:48], o_q_gain[0:1, 80:96])
        row(rows[G_OQO:G_OQO + 1, 48:64], o_q_gain[0:1, 64:80])
        row(rows[G_OQO:G_OQO + 1, 64:128], o_q_gain[0:1, 0:64])
        for i in range(4):
            row(rows[G_KR:G_KR + 1, 32 * i:32 * i + 32], o_k_gain[0:1, 64:96])
            row(rows[G_KRS:G_KRS + 1, 32 * i:32 * i + 16], o_k_gain[0:1, 80:96])
            row(rows[G_KRS:G_KRS + 1, 32 * i + 16:32 * i + 32], o_k_gain[0:1, 64:80])
        assert n_gain[0] == GAIN_DMAS
        pool.dma_start(sinks[:, :], e_sinks[0:1, :].broadcast_to([P, HEADS])).then_inc(sinks_loaded, 16)
        for g in range(2):
            pool.dma_start(gate_bias[64 * g:64 * g + 64, :, :],
                           o_spatial_bias.rearrange("a (j g) i -> a g j i", g=2)[:, g]
                           .broadcast_to([64, 4, P])).then_inc(gate_bias_loaded, 16)

        for j in range(4):
            pool.wait_ge(conv_in_scaled, j + 1)
            pool.tensor_tensor(conv_h[:, j, :], conv_h[:, j, :], row_scale[:, :], ALU.mult).then_inc(conv_in_ready, 1)
        for j in range(4):
            pool.wait_ge(conv_tap_c, j + 1)
            pool.tensor_tensor(conv_y[:, j, :], conv_y[:, j, :], row_scale[:, :], ALU.mult).then_inc(conv_y_scaled, 1)

        def scale_silus(layer):
            with pool.Fori(0, NG_FF // 2) as i:
                for t in range(4):
                    pool.wait_ge(silu_done, 22 * layer + t + 1 + 4 * i)
                    pool.tensor_tensor(ffn_t[:, t, :], ffn_t[:, t, :], row_scale[:, :], ALU.mult).then_inc(silu_scaled, 1)
            for t in range(2):
                pool.wait_ge(silu_done, 22 * layer + 20 + t + 1)
                pool.tensor_tensor(ffn_t[:, t, :], ffn_t[:, t, :], row_scale[:, :], ALU.mult).then_inc(silu_scaled, 1)

        scale_silus(0)
        pool.wait_ge(load_used, FFN_OUT[0] + 22)
        pool.memset(w_sp[0:64, :, 64:128], 0.0).then_inc(spatial_zeroed, 1)
        for j in range(4):
            n = O_CKV + j
            pool.wait_ge(raw_landed[n % 2], landed(n))
            v = raw[:, n % 2, :].rearrange("p (k n) -> p k n", k=2)
            for k in range(2):
                one = v[:, k, 256:288].unsqueeze(1)
                pool.tensor_copy(v[:, k, 288:384].rearrange("p (r c) -> p r c", r=3), one.broadcast_to([P, 3, 32]))
                sw = v[:, k, 384:512].rearrange("p (r c) -> p r c", r=4)
                pool.tensor_copy(sw[:, :, 0:16], one[:, :, 16:32].broadcast_to([P, 4, 16]))
                ins = pool.tensor_copy(sw[:, :, 16:32], one[:, :, 0:16].broadcast_to([P, 4, 16]))
            ins.then_inc(kr_columns, 1)
        for j in range(4):
            n = O_UQ + j
            pool.wait_ge(raw_landed[n % 2], landed(n))
            v = raw[:, n % 2, 0:768].rearrange("p (k n) -> p k n", k=3)
            for o in (64, 128):
                pool.tensor_copy(v[:, :, o + 32:o + 48], v[:, :, o + 16:o + 32])
                ins = pool.tensor_copy(v[:, :, o + 48:o + 64], v[:, :, o:o + 16])
            ins.then_inc(uq_columns, 1)
        pool.wait_ge(kr_rotated, 1)
        pool.wait_ge(uq_columns, 4)
        for n, h in enumerate((0, 2, 4, 6, 1, 3, 5, 7)):
            a = 64 * (1 - h % 2)
            if n == 4:
                pool.wait_ge(kr_copied, 4)
            pool.tensor_copy(o_k[a:a + 64, h, :], kr[a:a + 64, 0, :]).then_inc(kr_copied, 1)
        pool.wait_ge(kr_copied, HEADS)
        scale_silus(1)

    def g_col(i, a=0, b=P):
        return gains[a:b, i:i + 1]

    def h_gain(rnd, ft):
        return mix0_gain[:, ft:ft + 1] if rnd == 0 else g_col({1: G_FFN0, 2: G_MIX1, 3: G_FFN1}[rnd] + ft)

    def used_before(m):
        return sum(1 for i in range(m + 1) if i not in TO_ROW_SCALE)

    SCORE_ORDER = (3, 2, 0, 1)

    def score(i):
        bank, c0 = ((1, 384), (2, 0), (1, 0), (0, 0))[i]
        return ps[:, bank, c0:c0 + P * (i + 1)]

    @block.scalar
    def _(act):
        act.dma_start(mix0_gain[:, :], mix_norm[0].rearrange("(t p) -> p t", p=P), allow_slow_non_contiguous=True).then_inc(mix0_loaded, 16)
        act.dma_start(tables[:, :], c_tables).then_inc(tables_loaded, 16)
        act.dma_start(alibi[:, :, :], c_alibi.rearrange("p (h k) -> p h k", h=HEADS)).then_inc(alibi_loaded, 16)

        nxt = [0]

        def hi(n, shift=0, count=None):
            s = n % W_SLOTS
            if n >= W_SLOTS:
                act.wait_ge(load_used, n - W_SLOTS + 1 + shift)
            if count is None:
                act.wait_ge(raw_landed[n % 2], landed(n))
            else:
                act.wait_ge(raw_landed[n % 2], count)
            if O_CKV <= n < O_CV:
                act.wait_ge(kr_columns, n - O_CKV + 1)
            if O_UQ <= n < O_UKV:
                act.wait_ge(uq_columns, n - O_UQ + 1)
            pairs = list(zip(ordered(n, w_hi[:, s, :], None), ordered(n, None, raw[:, n % 2, :])))
            for dst, src in pairs:
                ins = act.activation(dst, src, ACT.Copy)
            ins.then_inc(hi_done, 1)

        def through(p):
            while nxt[0] <= min(p + LEAD, N_LOADS - 1):
                hi(nxt[0])
                nxt[0] += 1

        def fin(rnd, ft):
            f = 8 * rnd + ft
            act.wait_ge(x_ready, f + 1)
            act.activation(h_hi[:, ft, :], xT[:, ft, :], ACT.Copy, scale=h_gain(rnd, ft)).then_inc(h_hi_ready, 1)
            if ft >= 2:
                act.wait_ge(h_summed, f - 1)
            act.activation(sq[:, ft % 2, :], xT[:, ft, :], ACT.Square).then_inc(h_squared, 1)

        def rms(m, src, n):
            act.wait_ge(sums_ready, m + 1)
            if m >= 2:
                act.wait_ge(rs_ready, m - 1)
            act.activation(y0[:, m % 2, :], src, ACT.Abs_reciprocal_sqrt, bias=eps_col[:, :], scale=1.0 / n
                           ).then_inc(rs_first, 1)
            if m >= 2 and used_before(m - 2):
                act.wait_ge(rs_used, used_before(m - 2))
            act.wait_ge(rs_first, m + 1)
            act.activation(rs[:, m % 2, :], y0[:, m % 2, :], ACT.Square, scale=float((0.5 / n) ** 0.5)
                           ).then_inc(rs_square, 1)

        act.wait_ge(mix0_loaded, 16)
        act.wait_ge(columns_set, 1)
        for ft in range(DT):
            fin(0, ft)
            if ft % 2:
                hi(nxt[0])
                nxt[0] += 1
        through(1)
        rms(M_MIX0, ps[:, 4, :], D)
        through(3)
        for j in range(4):
            act.wait_ge(e_q_scaled, j + 1)
            act.activation(yb[:, j, :], e_q[:, j, :], ACT.Square).then_inc(e_q_squared, 1)
        through(4)
        act.wait_ge(gains_turned, 1)
        act.activation(gains[:, :], ps[:, 7, 0:N_GAINS], ACT.Copy).then_inc(gains_ready, 1)
        through(5)
        act.wait_ge(e_k_scaled, 1)
        act.activation(sq[:, 0, :], e_k[:, :], ACT.Square).then_inc(e_k_squared, 1)
        rms(M_EQ, ps[:, 6, :], 1)
        rms(M_EQ + 1, ps[:, 7, :], 1)
        through(6)
        rms(M_EQ + 2, ps[:, 6, :], 1)
        rms(M_EQ + 3, ps[:, 7, :], 1)
        through(7)
        rms(M_EK, ps[:, 4, :], 1)
        act.wait_ge(e_v_turned, 1)
        act.activation(e_v[:, :, :], ps[:, 5, :].rearrange("p (t c) -> p t c", t=QT), ACT.Copy).then_inc(e_v_ready, 1)
        def e_exp(i):
            lo, o = (128 if i == 0 else 0), 8 * (i % 2)
            act.wait_ge(a_neg_max, i + 1)
            act.wait_ge(a_sink_diff, i + 1)
            for h in range(HEADS):
                act.activation(e_sc[:, i % 2, h, lo:], e_sc[:, i % 2, h, lo:], ACT.Exp,
                               bias=tiny[:, o + 1, h:h + 1],
                               accum_out=tiny[:, o + 3, h:h + 1]).then_inc(a_exp_done, 1)
            act.activation(tiny[:, o + 4, :], tiny[:, o + 2, :], ACT.Exp).then_inc(a_sink_exp, 1)

        def e_out(i):
            act.wait_ge(a_values, i + 1)
            act.activation(yb[:, :, i * P:(i + 1) * P], ps[:, 4, :].rearrange("p (j q) -> p j q", j=4), ACT.Copy
                           ).then_inc(a_out, 1)
            act.wait_ge(a_out, i + 1)
            if i >= 2:
                act.wait_ge(yb_summed, i - 1)
            act.activation(sq[:, i % 2, :].rearrange("p (j q) -> p j q", j=4), yb[:, :, i * P:(i + 1) * P], ACT.Square
                           ).then_inc(yb_squared, 1)

        through(8)
        e_exp(0)
        through(10)
        act.wait_ge(a_probs_turned, 1)
        for kv in range(2):
            act.activation(e_pT[:, 2 * kv + 1, :], ps[:, 5 + 2 * kv, :], ACT.Copy).then_inc(a_pT_act, 1)
        e_exp(1)
        through(11)
        e_out(0)
        through(12)
        e_exp(2)
        through(13)
        e_out(1)
        for j in range(4):
            act.wait_ge(conv_h_ready, j + 1)
            act.activation(conv_y[:, j, :], conv_h[:, j, :], ACT.Copy, scale=g_col(G_CONV + 8 + j)).then_inc(conv_tap_a, 1)
        e_exp(3)
        through(14)
        e_out(2)
        through(15)
        e_out(3)
        through(16)
        rms(M_EB, ps[:, 5, :], 512)
        for j in range(4):
            act.wait_ge(yb_normed, j + 1)
            act.activation(yb_hi[:, j, :], yb[:, j, :], ACT.Copy).then_inc(yb_hi_ready, 1)
        through(17)
        for j in range(4):
            act.wait_ge(ya_ready, j + 1)
            if j >= 2:
                act.wait_ge(ya_summed, j - 1)
            act.activation(sq[:, j % 2, :], conv_y[:, j, :], ACT.Square).then_inc(ya_squared, 1)
        through(18)
        rms(M_EA, ps[:, 0, :], 512)
        for j in range(4):
            act.wait_ge(ya_normed, j + 1)
            act.activation(ya_hi[:, j, :], conv_y[:, j, :], ACT.Copy).then_inc(ya_hi_ready, 1)

        def residual(rnd, out0):
            through(out0 + 3)
            for ft in range(4):
                fin(rnd, ft)
            through(out0 + 7)
            for ft in range(4, 8):
                fin(rnd, ft)


        def ffn(layer, bank0):
            n0, n1 = FFN_IN[layer], FFN_OUT[layer]
            c = 22 * layer
            through(n0 + 1)
            rms(M_FFN0 if layer == 0 else M_FFN1, ps[:, (1 - bank0) * 4, :], D)
            through(n0 + 3)

            def group(t0, dst, shift):
                for t in range(2):
                    act.wait_ge(gate_scaled, c + t0 + t + 1 + shift)
                    b = (t0 + t) % 4
                    act.activation(ffn_t[:, b, :], ffn_t[:, b, :], ACT.Silu).then_inc(silu_done, 1)
                for t in range(2):
                    act.wait_ge(hidden_ready, 1 + c + t0 + t + 1 + shift)
                    act.activation(dst[:, t, :], ffn_t[:, (t0 + t) % 4, :], ACT.Copy).then_inc(hidden_hi, 1)

            group(0, act_hi[:, 0:2, :], 0)
            with act.Fori(0, NG_FF // 2) as i:
                for g in (1, 2):
                    for j in range(4):
                        n = n0 + 4 * g + 4 + j
                        hi(n, 8 * i, landed(n) + 64 * i)
                    group(2 * g, act_hi[:, bass.ds(4 * i + 2 * g, 2), :], 4 * i)
            nxt[0] = n1 + 4
            n = nxt[0]
            through(n1 + 2)
            with act.Fori(0, 2) as i:
                for j in range(4):
                    hi(n + 3 + j, 4 * i, landed(n + 3 + j) + 32 * i)
            nxt[0] = n + 11

        residual(1, E_OUT)
        ffn(0, 1)
        for ft in range(4):
            fin(2, ft)
        through(FFN_OUT[0] + 21)
        for ft in range(4, 8):
            fin(2, ft)

        through(O_CQ + 1)
        rms(M_MIX1, ps[:, 4, :], D)
        act.wait_ge(tok_sums, 1)
        act.activation(tiny[:, 0, 0:4], ps[:, 5, 0:4], ACT.Abs_reciprocal_sqrt, bias=eps_col[:, :], scale=1.0 / D
                       ).then_inc(tok_first, 1)
        act.wait_ge(tok_first, 1)
        act.activation(tiny[:, 5, 0:4], tiny[:, 0, 0:4], ACT.Square, scale=float((0.5 / D) ** 0.5)
                       ).then_inc(tok_square, 1)
        through(O_CQ + 3)
        for j in range(3):
            act.wait_ge(cq_scaled, j + 1)
            if j >= 2:
                act.wait_ge(cq_summed, j - 1)
            act.activation(sq[:, j % 2, :], cq[:, j, :], ACT.Square).then_inc(cq_squared, 1)
        through(O_CQ + 4)
        rms(M_CQ, ps[:, 3, :], 384)
        for j in range(3):
            act.wait_ge(cq_normed, j + 1)
            act.activation(cq_hi[:, j, :], cq[:, j, :], ACT.Copy).then_inc(cq_hi_ready, 1)
        through(O_CKV + 3)
        for j in range(2):
            act.wait_ge(ckv_scaled, j + 1)
            act.activation(sq[:, j, :], ckv[:, j, :], ACT.Square).then_inc(ckv_squared, 1)
        act.wait_ge(ckv_scaled, 3)
        act.wait_ge(ckv_summed, 2)
        act.activation(sq[:, 0, :], kr[:, 0, :], ACT.Square).then_inc(ckv_squared, 1)
        through(O_CV)
        rms(M_CKV, ps[:, 4, :], 256)
        for j in range(2):
            act.wait_ge(ckv_normed, j + 1)
            act.activation(ckv_hi[:, j, :], ckv[:, j, :], ACT.Copy).then_inc(ckv_hi_ready, 1)
        rms(M_KR, ps[:, 5, :], P)
        through(O_CV + 2)
        act.wait_ge(ckv_lo_ready, 2)
        for b in range(2):
            act.wait_ge(spatial_turned, b + 1)
            act.activation(w_spT[:, 4 * b:4 * b + 4, :], ps[:, 6 + b, :].rearrange("p (g i) -> p g i", g=4), ACT.Copy
                           ).then_inc(spatial_ready, 1)
        through(O_CV + 3)
        act.wait_ge(tok_scale, 1)
        act.wait_ge(load_used, O_CV + 4)
        for t in range(QT):
            act.activation(v_c[:, t, :], ps[:, t, :], ACT.Gelu_apprx_tanh, scale=tiny[:, 6, t:t + 1]).then_inc(cv_ready, 1)
        for t in range(QT):
            act.wait_ge(cv_ready, t + 1)
            if t == 0:
                act.wait_ge(ckv_lo_ready, 2)
                act.wait_ge(sums_ready, M_KR + 1)
            if t >= 1:
                act.wait_ge(cv_squared, t)
            act.activation(sq[:, 0, :], v_c[:, t, :], ACT.Square, accum_out=tiny[:, 7, t:t + 1]).then_inc(cv_squared, 1)
        act.wait_ge(cv_squared, QT)
        act.activation(tiny[:, 8, 0:4], tiny[:, 7, 0:4], ACT.Abs_reciprocal_sqrt, bias=eps_col[:, :], scale=1.0 / 512
                       ).then_inc(cv_first, 1)
        act.wait_ge(cv_first, 1)
        act.activation(tiny[:, 13, 0:4], tiny[:, 8, 0:4], ACT.Square, scale=float((0.5 / 512) ** 0.5)
                       ).then_inc(cv_square, 1)

        def q_squares(hs, b0):
            for j, h in enumerate(hs):
                if h >= 2:
                    act.wait_ge(sums_ready, M_OQ + h - 1)
                act.activation(sq[:, h % 2, :], ps[:, b0 + j, :], ACT.Square).then_inc(oq_squared, 1)

        through(O_UQ + 1)
        act.wait_ge(load_used, O_UQ + 2)
        q_squares(range(4), 4)
        through(O_UQ + 2)
        for j in range(4):
            rms(M_OQ + j, ps[:, 4 + j, :], 1)
        through(O_UQ + 3)
        act.wait_ge(load_used, O_UQ + 4)
        q_squares(range(4, 8), 0)
        through(O_UKV)
        for j in range(4):
            rms(M_OQ + 4 + j, ps[:, j, :], 1)

        def kv_tiles(half, b0):
            act.wait_ge(load_used, O_UKV + half + 1)
            for j in range(2):
                act.wait_ge(sums_ready, M_OK + 2 * half + j - 1)
                act.activation(sq[:, j, :], ps[:, b0 + j, :], ACT.Square).then_inc(ok_squared, 1)
            act.activation(o_v[:, 0:2, 256 * half:256 * half + 256],
                           ps[:, b0 + 2, :].rearrange("p (t c) -> p t c", t=2), ACT.Copy).then_inc(ov_act, 1)

        kv_tiles(0, 4)
        through(O_UKV + 1)
        for j in range(2):
            rms(M_OK + j, ps[:, 4 + j, :], 1)
        kv_tiles(1, 0)
        through(O_CU)
        for j in range(2):
            rms(M_OK + 2 + j, ps[:, j, :], 1)
        through(O_CU + 3)
        for j in range(4):
            act.wait_ge(u_scaled, j + 1)
            act.activation(u_c[:, j, :], u_c[:, j, :], ACT.Gelu_apprx_tanh).then_inc(u_ready, 1)
        for j in range(4):
            act.wait_ge(yc_ready, j + 1)
            if j >= 2:
                act.wait_ge(yc_summed, j - 1)
            act.activation(sq[:, j % 2, :], yc[:, j, :], ACT.Square).then_inc(yc_squared, 1)
        rms(M_OC, ps[:, 3, :], 512)
        for j in range(4):
            act.wait_ge(yc_normed, j + 1)
            act.activation(yc_hi[:, j, :], yc[:, j, :], ACT.Copy).then_inc(yc_hi_ready, 1)
        def o_exp(h):
            o = 8 * (h % 2)
            if h == 0:
                act.wait_ge(yc_lo_ready, 4)
            if h >= 2:
                act.wait_ge(d_probs_turned, h - 1)
            act.wait_ge(d_neg_max, h + 1)
            for i in SCORE_ORDER:
                act.activation(o_p[:, h % 2, i, 0:P * (i + 1)], score(i), ACT.Exp,
                               bias=tiny[:, o + 1, i:i + 1], scale=O_SCALE,
                               accum_out=tiny[:, o + 2, i:i + 1]).then_inc(d_exp_done, 1)

        def o_out(h):
            a, j = 64 * (h % 2), h // 2
            act.wait_ge(d_values, h + 1)
            act.activation(yd[a:a + 64, j, :], ps[a:a + 64, 7, :], ACT.Copy).then_inc(d_out, 1)
            if h % 2:
                act.wait_ge(d_out, h + 1)
                if j >= 2:
                    act.wait_ge(yd_summed, j - 1)
                act.activation(sq[:, j % 2, :], yd[:, j, :], ACT.Square).then_inc(yd_squared, 1)

        o_exp(0)
        for h in range(HEADS):
            if h + 1 < HEADS:
                o_exp(h + 1)
            if h >= 1:
                o_out(h - 1)
            act.wait_ge(d_probs_turned, h + 1)
            act.activation(o_pT[:, 0, :], ps[:, 4, :], ACT.Copy).then_inc(d_pT_act, 1)
            act.activation(o_pT[:, 2, 0:256], ps[:, 6, 0:256], ACT.Copy).then_inc(d_pT_act, 1)
        o_out(7)
        through(O_OUT)
        rms(M_OD, ps[:, 4, :], 512)
        for j in range(4):
            act.wait_ge(yd_normed, j + 1)
            act.activation(yd_hi[:, j, :], yd[:, j, :], ACT.Copy).then_inc(yd_hi_ready, 1)
        residual(3, O_OUT)
        ffn(1, 0)
        for half in range(2):
            if half:
                through(N_LOADS - 1)
            for t in (0, 2):
                b0 = 4 if half == 0 else 0
                act.wait_ge(out_turned, 4 * half + t + 1)
                act.activation(out_tok[:, t, 512 * half:512 * half + 512], ps[:, b0 + t, :], ACT.Copy).then_inc(out_act, 1)

    @block.vector
    def _(dve):
        TT, STT, TS, TC = dve.tensor_tensor, dve.scalar_tensor_tensor, dve.tensor_scalar, dve.tensor_copy
        nxt = [0]

        def lo(n, shift=0):
            s = n % W_SLOTS
            dve.wait_ge(hi_done, n + 1 + shift)
            parts = zip(ordered(n, w_lo[:, s, :], None), ordered(n, None, raw[:, n % 2, :]),
                        ordered(n, w_hi[:, s, :].bitcast(F32), None))
            for dst, src, high in parts:
                ins = TT(dst, src, high, ALU.subtract)
            ins.then_inc(lo_done, 1)

        def through(p):
            while nxt[0] <= min(p + LEAD, N_LOADS - 1):
                lo(nxt[0])
                nxt[0] += 1

        def low(dst, src, high, done):
            TT(dst, src, high.bitcast(F32), ALU.subtract).then_inc(done, 1)

        def fin(rnd, ft):
            f = 8 * rnd + ft
            dve.wait_ge(h_hi_ready, f + 1)
            STT(out=h_lo[:, ft, :], in0=xT[:, ft, :], scalar=h_gain(rnd, ft), in1=h_hi[:, ft, :].bitcast(F32),
                op0=ALU.mult, op1=ALU.subtract).then_inc(h_lo_ready, 1)
            dve.wait_ge(h_squared, f + 1)
            if ft == 0:
                if rnd:
                    dve.wait_ge(sums_ready, (M_MIX0, M_EA, M_FFN0, M_OD)[rnd] + 1)
                TC(acc[:, :], sq[:, 0, :]).then_inc(h_summed, 1)
            else:
                dve.wait_ge(h_summed, f)
                TT(acc[:, :], acc[:, :], sq[:, ft % 2, :], ALU.add).then_inc(h_summed, 1)

        def sum_squares(squared, summed, count, read_by):
            for j in range(count):
                dve.wait_ge(squared, j + 1)
                if j == 0:
                    dve.wait_ge(sums_ready, read_by + 1)
                    TC(acc[:, :], sq[:, 0, :]).then_inc(summed, 1)
                else:
                    dve.wait_ge(summed, j)
                    TT(acc[:, :], acc[:, :], sq[:, j % 2, :], ALU.add).then_inc(summed, 1)

        def rms(m, src, n):
            b = m % 2
            dve.wait_ge(rs_square, m + 1)
            STT(out=rs[:, b, :], in0=src, scalar=n * EPS, in1=rs[:, b, :], op0=ALU.add, op1=ALU.mult
                ).then_inc(rs_step, 1)
            dve.wait_ge(rs_step, m + 1)
            dst = row_scale[:, :] if m in TO_ROW_SCALE else rs[:, b, :]
            STT(out=dst, in0=rs[:, b, :], scalar=1.5, in1=y0[:, b, :], op0=ALU.subtract, op1=ALU.mult, reverse0=True
                ).then_inc(rs_ready, 1)
            dve.wait_ge(rs_ready, m + 1)
            return rs[:, b, :]

        def normed(tiles, gain0, r, count, done, high, low_, high_done, low_done):
            for j0 in range(0, count, 2):
                two = range(j0, min(j0 + 2, count))
                for j in two:
                    STT(out=tiles[:, j, :], in0=tiles[:, j, :], scalar=g_col(gain0 + j), in1=r,
                        op0=ALU.mult, op1=ALU.mult).then_inc(done, 1)
                for j in two:
                    dve.wait_ge(high_done, j + 1)
                    low(low_[:, j, :], tiles[:, j, :], high[:, j, :], low_done)
            dve.sem_inc(rs_used, 1)

        dve.sem_inc(hidden_ready, 1)
        dve.wait_ge(small_loaded, 16)
        for ft in range(DT):
            dve.wait_ge(x_turned, ft + 1)
            TC(xT[:, ft, :], ps[:, ft, :]).then_inc(x_ready, 1)
            if ft >= 1:
                fin(0, ft - 1)
            if ft % 2 == 0 and ft:
                lo(nxt[0])
                nxt[0] += 1
        fin(0, 7)
        through(1)
        rms(M_MIX0, ps[:, 4, :], D)
        through(3)
        dve.wait_ge(load_used, E_Q + 4)
        for j in range(4):
            TT(e_q[:, j, :], ps[:, j, :], row_scale[:, :], ALU.mult).then_inc(e_q_scaled, 1)
        through(5)
        dve.wait_ge(load_used, E_KV + 2)
        TT(e_k[:, :], ps[:, 4, :], row_scale[:, :], ALU.mult).then_inc(e_k_scaled, 1)
        TT(e_vT[:, :], ps[:, 5, :], row_scale[:, :], ALU.mult).then_inc(e_v_scaled, 1)

        def e_norm(m, bank, tile, gain, extra):
            r = rms(m, ps[:, bank, :], 1)
            STT(out=tile, in0=tile, scalar=g_col(gain), in1=r, op0=ALU.mult, op1=ALU.mult).then_inc(rs_used, 1)

        dve.wait_ge(gains_ready, 1)
        e_norm(M_EQ, 6, e_q[:, 0, :], G_EQ, 1)
        e_norm(M_EQ + 1, 7, e_q[:, 1, :], G_EQ, 1)
        through(6)
        e_norm(M_EQ + 2, 6, e_q[:, 2, :], G_EQ, 1)
        e_norm(M_EQ + 3, 7, e_q[:, 3, :], G_EQ, 1)
        through(7)
        e_norm(M_EK, 4, e_k[:, :], G_EK, 1)
        dve.wait_ge(alibi_loaded, 16)
        dve.wait_ge(sinks_loaded, 16)

        def e_max(i):
            lo_, o, b0 = (128 if i == 0 else 0), 8 * (i % 2), 4
            dve.wait_ge(a_scores, i + 1)
            if i >= 2:
                dve.wait_ge(a_probs_turned, i - 1)
            sc = e_sc[:, i % 2]
            for b in range(4):
                STT2(sc[:, 2 * b:2 * b + 2, lo_:], ps[:, b0 + b, :].rearrange("p (h k) -> p h k", h=2)[:, :, lo_:],
                     alibi[:, 2 * b:2 * b + 2, lo_:])
            dve.wait_ge(a_biased, 4 * (i + 1))
            dve.tensor_reduce(tiny[:, o, :], sc[:, :, lo_:], AX, ALU.max).then_inc(a_row_max, 1)
            dve.wait_ge(a_row_max, i + 1)
            TT(tiny[:, o, :], tiny[:, o, :], sinks[:, :], ALU.max).then_inc(a_max, 1)
            dve.wait_ge(a_max, i + 1)
            TS(tiny[:, o + 1, :], tiny[:, o, :], -1.0, None, ALU.mult).then_inc(a_neg_max, 1)
            TT(tiny[:, o + 2, :], sinks[:, :], tiny[:, o, :], ALU.subtract).then_inc(a_sink_diff, 1)

        def STT2(dst, scores, penalty):
            STT(out=dst, in0=scores, scalar=E_SCALE, in1=penalty, op0=ALU.mult, op1=ALU.add).then_inc(a_biased, 1)

        def e_prob(i):
            lo_, o = (128 if i == 0 else 0), 8 * (i % 2)
            dve.wait_ge(a_sink_exp, i + 1)
            TT(tiny[:, o + 5, :], tiny[:, o + 3, :], tiny[:, o + 4, :], ALU.add).then_inc(a_denominator, 1)
            dve.wait_ge(a_denominator, i + 1)
            dve.reciprocal(tiny[:, o + 6, :], tiny[:, o + 5, :]).then_inc(a_inverse, 1)
            dve.wait_ge(a_inverse, i + 1)
            for h in range(HEADS):
                TS(e_sc[:, i % 2, h, lo_:], e_sc[:, i % 2, h, lo_:], tiny[:, o + 6, h:h + 1], None, ALU.mult
                   ).then_inc(a_probs, 1)

        def e_pt(i):
            dve.wait_ge(a_probs_turned, i + 1)
            dve.wait_ge(a_values, i)
            for b in range(4):
                TC(e_pT[:, b, :], ps[:, 4 + b, :]).then_inc(a_pT_dve, 1)

        def e_sum(i):
            dve.wait_ge(yb_squared, i + 1)
            dve.tensor_reduce(acc[:, i * P:(i + 1) * P], sq[:, i % 2, :].rearrange("p (j q) -> p q j", j=4), AX, ALU.add
                              ).then_inc(yb_summed, 1)

        through(8)
        e_max(0)
        dve.wait_ge(load_used, E_AIN + 4)
        for j in range(4):
            TT(conv_h[:, j, :], ps[:, j, :], row_scale[:, :], ALU.mult).then_inc(conv_in_scaled, 1)
        e_prob(0)
        through(9)
        e_max(1)
        through(10)
        e_prob(1)
        through(11)
        dve.wait_ge(sums_ready, M_MIX0 + 1)
        e_sum(0)
        e_max(2)
        e_pt(1)
        through(12)
        e_prob(2)
        dve.wait_ge(load_used, E_AC + 4)
        for j in range(4):
            dve.wait_ge(conv_in_ready, j + 1)
            TT(conv_h[:, j, :], ps[:, j, :], conv_h[:, j, :], ALU.mult).then_inc(conv_h_ready, 1)
        through(13)
        e_sum(1)
        e_max(3)
        for j in range(4):
            dve.wait_ge(conv_tap_a, j + 1)
            STT(out=conv_y[:, j, 1:], in0=conv_h[:, j, 0:S - 1], scalar=g_col(G_CONV + 4 + j), in1=conv_y[:, j, 1:],
                op0=ALU.mult, op1=ALU.add).then_inc(conv_tap_b, 1)
        e_pt(2)
        e_prob(3)
        through(14)
        for j in range(4):
            dve.wait_ge(conv_tap_b, j + 1)
            STT(out=conv_y[:, j, 2:], in0=conv_h[:, j, 0:S - 2], scalar=g_col(G_CONV + j), in1=conv_y[:, j, 2:],
                op0=ALU.mult, op1=ALU.add).then_inc(conv_tap_c, 1)
        e_pt(3)
        e_sum(2)
        through(15)
        e_sum(3)
        through(16)
        r = rms(M_EB, ps[:, 5, :], 512)
        normed(yb, G_EB, r, 4, yb_normed, yb_hi, yb_lo, yb_hi_ready, yb_lo_ready)
        dve.wait_ge(load_used, E_AB + 4)
        for j in range(4):
            dve.wait_ge(conv_y_scaled, j + 1)
            TT(conv_y[:, j, :], ps[:, j, :], conv_y[:, j, :], ALU.mult).then_inc(ya_ready, 1)
        through(17)
        sum_squares(ya_squared, ya_summed, 4, M_EB)
        through(18)
        r = rms(M_EA, ps[:, 0, :], 512)
        normed(conv_y, G_EA, r, 4, ya_normed, ya_hi, ya_lo, ya_hi_ready, ya_lo_ready)

        def add_x(rnd, last_load, ft0, bank0):
            dve.wait_ge(load_used, last_load + 1)
            for j in range(4):
                TT(xT[:, ft0 + j, :], ps[:, bank0 + j, :], xT[:, ft0 + j, :], ALU.add).then_inc(x_ready, 1)
                if 0 < j and rnd < 4:
                    fin(rnd, ft0 + j - 1)
            if rnd < 4:
                fin(rnd, ft0 + 3)

        def residual(rnd, out0, bank0):
            through(out0 + 3)
            add_x(rnd, out0 + 3, 0, bank0)
            through(out0 + 7)
            add_x(rnd, out0 + 7, 4, 4 - bank0)

        def ffn(layer, bank0):
            n0, n1 = FFN_IN[layer], FFN_OUT[layer]
            c = 22 * layer
            through(n0 + 1)
            rms(M_FFN0 if layer == 0 else M_FFN1, ps[:, (1 - bank0) * 4, :], D)
            through(n0 + 3)

            def group(t0, b0, load, dst_hi, dst_lo, shift, load_shift):
                dve.wait_ge(load_used, load + 4 + load_shift)
                for t in range(2):
                    TT(ffn_t[:, (t0 + t) % 4, :], ps[:, b0 + t, :], row_scale[:, :], ALU.mult).then_inc(gate_scaled, 1)
                for t in range(2):
                    b = (t0 + t) % 4
                    dve.wait_ge(silu_scaled, c + t0 + t + 1 + shift)
                    TT(ffn_t[:, b, :], ps[:, b0 + 2 + t, :], ffn_t[:, b, :], ALU.mult).then_inc(hidden_ready, 1)
                for t in range(2):
                    dve.wait_ge(hidden_hi, c + t0 + t + 1 + shift)
                    TT(dst_lo[:, t, :], ffn_t[:, (t0 + t) % 4, :], dst_hi[:, t, :].bitcast(F32), ALU.subtract
                       ).then_inc(hidden_lo, 1)

            group(0, 4 * bank0, n0, act_hi[:, 0:2, :], act_lo[:, 0:2, :], 0, 0)
            with dve.Fori(0, NG_FF // 2) as i:
                for g in (1, 2):
                    for j in range(4):
                        lo(n0 + 4 * g + 4 + j, 8 * i)
                    t = bass.ds(4 * i + 2 * g, 2)
                    group(2 * g, 4 * ((bank0 + g) % 2), n0 + 4 * g, act_hi[:, t, :], act_lo[:, t, :], 4 * i, 8 * i)
            nxt[0] = n1 + 4
            n = nxt[0]
            through(n1 + 2)
            with dve.Fori(0, 2) as i:
                for j in range(4):
                    lo(n + 3 + j, 4 * i)
            nxt[0] = n + 11

        residual(1, E_OUT, 4)
        ffn(0, 1)
        add_x(2, FFN_OUT[0] + 10, 0, 0)
        through(FFN_OUT[0] + 21)
        add_x(2, FFN_OUT[0] + 21, 4, 4)

        through(O_CQ + 1)
        rms(M_MIX1, ps[:, 4, :], D)
        dve.wait_ge(tok_square, 1)
        STT(out=tiny[:, 5, 0:4], in0=ps[:, 5, 0:4], scalar=D * EPS, in1=tiny[:, 5, 0:4], op0=ALU.add, op1=ALU.mult
            ).then_inc(tok_step, 1)
        dve.wait_ge(tok_step, 1)
        STT(out=tiny[:, 6, 0:4], in0=tiny[:, 5, 0:4], scalar=1.5, in1=tiny[:, 0, 0:4], op0=ALU.subtract, op1=ALU.mult,
            reverse0=True).then_inc(tok_scale, 1)
        through(O_CQ + 3)
        dve.wait_ge(load_used, O_CQ + 4)
        for j in range(3):
            TT(cq[:, j, :], ps[:, j, :], row_scale[:, :], ALU.mult).then_inc(cq_scaled, 1)
        sum_squares(cq_squared, cq_summed, 3, M_MIX1)
        through(O_CQ + 4)
        r = rms(M_CQ, ps[:, 3, :], 384)
        normed(cq, G_CQ, r, 3, cq_normed, cq_hi, cq_lo, cq_hi_ready, cq_lo_ready)
        through(O_CKV + 3)
        dve.wait_ge(load_used, O_CKV + 4)
        for j in range(2):
            TT(ckv[:, j, :], ps[:, 4 + j, :], row_scale[:, :], ALU.mult).then_inc(ckv_scaled, 1)
        for j in range(2):
            TT(kr[:, j, :], ps[:, 6 + j, :], row_scale[:, :], ALU.mult).then_inc(ckv_scaled, 1)
        sum_squares(ckv_squared, ckv_summed, 2, M_CQ)
        through(O_CV)
        r = rms(M_CKV, ps[:, 4, :], 256)
        normed(ckv, G_CKV, r, 2, ckv_normed, ckv_hi, ckv_lo, ckv_hi_ready, ckv_lo_ready)
        r = rms(M_KR, ps[:, 5, :], P)
        dve.wait_ge(tables_loaded, 16)
        STT(out=kr[:, 0, :], in0=kr[:, 0, :], scalar=g_col(G_KR), in1=r, op0=ALU.mult, op1=ALU.mult).then_inc(kr_normed, 1)
        STT(out=kr[:, 1, :], in0=kr[:, 1, :], scalar=g_col(G_KRS), in1=r, op0=ALU.mult, op1=ALU.mult).then_inc(kr_normed, 1)
        dve.wait_ge(kr_normed, 2)
        TT(kr[:, 0, :], kr[:, 0, :], tables[:, TAB_C:TAB_C + S], ALU.mult).then_inc(kr_turning, 1)
        TT(kr[:, 1, :], kr[:, 1, :], tables[:, TAB_S:TAB_S + S], ALU.mult).then_inc(kr_turning, 1)
        dve.sem_inc(rs_used, 1)
        dve.wait_ge(kr_turning, 2)
        TT(kr[:, 0, :], kr[:, 0, :], kr[:, 1, :], ALU.add).then_inc(kr_rotated, 1)
        through(O_CV + 3)
        dve.wait_ge(cv_square, 1)
        TS(tiny[:, 7, 0:4], tiny[:, 7, 0:4], 512 * EPS, None, ALU.add).then_inc(cv_step, 1)
        dve.wait_ge(cv_step, 1)
        TT(tiny[:, 13, 0:4], tiny[:, 7, 0:4], tiny[:, 13, 0:4], ALU.mult).then_inc(cv_step, 1)
        dve.wait_ge(cv_step, 2)
        STT(out=tiny[:, 15, 0:4], in0=tiny[:, 13, 0:4], scalar=1.5, in1=tiny[:, 8, 0:4], op0=ALU.subtract, op1=ALU.mult,
            reverse0=True).then_inc(cv_scale, 1)
        dve.wait_ge(cv_scale, 1)
        for t in range(QT):
            TS(v_c[:, t, :], v_c[:, t, :], tiny[:, 15, t:t + 1], None, ALU.mult).then_inc(cv_normed, 1)

        def q_tiles(hs, b0):
            for j, h in enumerate(hs):
                dve.wait_ge(oq_squared, h + 1)
                tab = TAB_ODD if h % 2 else TAB_EVEN
                STT(out=o_q[:, h, :], in0=ps[:, b0 + j, :], scalar=g_col(G_OQO if h % 2 else G_OQE),
                    in1=tables[:, tab:tab + S], op0=ALU.mult, op1=ALU.mult).then_inc(oq_turned, 1)

        def q_norm(hs, b0):
            for j, h in enumerate(hs):
                r = rms(M_OQ + h, ps[:, b0 + j, :], 1)
                TT(o_q[:, h, :], o_q[:, h, :], r, ALU.mult).then_inc(rs_used, 1)

        through(O_UQ + 1)
        q_tiles(range(4), 4)
        through(O_UQ + 2)
        q_norm(range(4), 4)
        through(O_UQ + 3)
        q_tiles(range(4, 8), 0)
        through(O_UKV)
        q_norm(range(4, 8), 0)

        def kv_tiles(half, b0):
            dve.wait_ge(load_used, O_UKV + half + 1)
            TC(o_v[:, 2:4, 256 * half:256 * half + 256], ps[:, b0 + 3, :].rearrange("p (t c) -> p t c", t=2)
               ).then_inc(ov_dve, 1)
            for j in range(2):
                dve.wait_ge(ok_squared, 2 * half + j + 1)
                TS(k_pair[:, 2 * half + j, :], ps[:, b0 + j, :], g_col(G_OK), None, ALU.mult).then_inc(ok_gained, 1)

        def k_norm(half, b0):
            for j in range(2):
                p = 2 * half + j
                r = rms(M_OK + p, ps[:, b0 + j, :], 1)
                dve.wait_ge(ok_gained, p + 1)
                TT(o_k[0:64, 2 * p, :], k_pair[0:64, p, :], r[0:64, :], ALU.mult).then_inc(ok_normed, 1)
                TT(o_k[64:128, 2 * p + 1, :], k_pair[64:128, p, :], r[64:128, :], ALU.mult).then_inc(rs_used, 1)

        kv_tiles(0, 4)
        through(O_UKV + 1)
        k_norm(0, 4)
        kv_tiles(1, 0)
        through(O_CU)
        k_norm(1, 0)
        through(O_CU + 1)
        dve.wait_ge(gate_bias_loaded, 32)
        dve.wait_ge(gates_mixed, 1)
        dve.wait_ge(kr_copied, HEADS)
        for j in range(4):
            STT(out=yc[:, j, :].rearrange("p (n i) -> p n i", n=QT), in0=ps[:, j, :].rearrange("p (n i) -> p n i", n=QT),
                scalar=g_col(G_V + j), in1=gate_bias[:, j:j + 1, :].broadcast_to([P, QT, P]),
                op0=ALU.mult, op1=ALU.add).then_inc(gates_ready, 1)
        through(O_CU + 3)
        dve.wait_ge(load_used, O_CU + 4)
        for j in range(4):
            TT(u_c[:, j, :], ps[:, 4 + j, :], row_scale[:, :], ALU.mult).then_inc(u_scaled, 1)
        dve.wait_ge(gates_ready, 4)
        for j in range(4):
            dve.wait_ge(u_ready, j + 1)
            TT(yc[:, j, :], yc[:, j, :], u_c[:, j, :], ALU.mult).then_inc(yc_ready, 1)
        sum_squares(yc_squared, yc_summed, 4, M_CKV)
        r = rms(M_OC, ps[:, 3, :], 512)
        normed(yc, G_OOUT, r, 4, yc_normed, yc_hi, yc_lo, yc_hi_ready, yc_lo_ready)

        def o_max(h):
            o = 8 * (h % 2)
            for n, i in enumerate(SCORE_ORDER):
                dve.wait_ge(d_scores, QT * h + (1, 3, 3, 4)[n])
                dve.tensor_reduce(tiny[:, o, i:i + 1], score(i), AX, ALU.max).then_inc(d_max, 1)
            dve.wait_ge(d_max, QT * (h + 1))
            TS(tiny[:, o + 1, 0:4], tiny[:, o, 0:4], -O_SCALE, None, ALU.mult).then_inc(d_neg_max, 1)

        def o_prob(h):
            o = 8 * (h % 2)
            dve.wait_ge(d_exp_done, QT * (h + 1))
            dve.reciprocal(tiny[:, o + 3, 0:4], tiny[:, o + 2, 0:4]).then_inc(d_inverse, 1)
            dve.wait_ge(d_inverse, h + 1)
            for i in range(QT):
                p = o_p[:, h % 2, i, 0:P * (i + 1)]
                TS(p, p, tiny[:, o + 3, i:i + 1], None, ALU.mult).then_inc(d_probs, 1)

        def yd_sum(j):
            dve.wait_ge(yd_squared, j + 1)
            if j:
                dve.wait_ge(yd_summed, j)
                TT(acc[:, :], acc[:, :], sq[:, j % 2, :], ALU.add).then_inc(yd_summed, 1)
            else:
                dve.wait_ge(sums_ready, M_OC + 1)
                TC(acc[:, :], sq[:, 0, :]).then_inc(yd_summed, 1)

        o_max(0)
        for h in range(HEADS):
            o_prob(h)
            if h + 1 < HEADS:
                o_max(h + 1)
            if h >= 3 and h % 2:
                yd_sum(h // 2 - 1)
            dve.wait_ge(d_probs_turned, h + 1)
            if h:
                dve.wait_ge(d_values, h)
            TC(o_pT[:, 1, :], ps[:, 5, :]).then_inc(d_pT_dve, 1)
        yd_sum(3)
        through(O_OUT)
        r = rms(M_OD, ps[:, 4, :], 512)
        normed(yd, G_OOUT + 4, r, 4, yd_normed, yd_hi, yd_lo, yd_hi_ready, yd_lo_ready)
        residual(3, O_OUT, 0)
        ffn(1, 0)
        for half in range(2):
            b0 = 4 if half == 0 else 0
            if half:
                through(N_LOADS - 1)
            add_x(4, FFN_OUT[1] + 10 + 11 * half, 4 * half, b0)
            for t in (1, 3):
                dve.wait_ge(out_turned, 4 * half + t + 1)
                TC(out_tok[:, t, 512 * half:512 * half + 512], ps[:, b0 + t, :]).then_inc(out_dve, 1)

    @block.tensor
    def _(pe):
        MM = pe.matmul

        def product(dst, st_hi, st_lo, mv_hi, mv_lo, start, stop):
            MM(dst, st_hi, mv_hi, start=start, stop=False)
            MM(dst, st_hi, mv_lo, start=False, stop=False)
            return MM(dst, st_lo, mv_hi, start=False, stop=stop)

        def ready(n, shift=0):
            pe.wait_ge(lo_done, n + 1 + shift)

        def load(n, tiles, ks, moving, banks, first, last, shift=0, extra=None):
            ready(n, shift)
            hi_, lo_ = w_hi[:, n % W_SLOTS, :], w_lo[:, n % W_SLOTS, :]
            for kk, k in enumerate(ks):
                if kk and extra:
                    extra()
                mh, ml = moving(k)
                th, tl = tiles(hi_, kk), tiles(lo_, kk)
                for t, b in enumerate(banks):
                    ins = product(ps[0:P, b, :], th[t], tl[t], mh, ml,
                                  first and kk == 0, last and kk == len(ks) - 1)
            ins.then_inc(load_used, 1)

        def plain(cols, count):
            return lambda w, kk: [w[:, cols * kk + P * t:cols * kk + P * t + P] for t in range(count)]

        H = lambda k: (h_hi[:, k, :], h_lo[:, k, :])

        def mean(m, bank, weights, src):
            MM(ps[:, bank, :], weights, src, start=True, stop=True).then_inc(sums_ready, 1)

        pe.wait_ge(small_loaded, 16)
        pe.wait_ge(x_loaded, 64)
        for ft in range(DT):
            for t in range(QT):
                ins = pe.transpose(ps[:, ft, t * P:(t + 1) * P], x_tok[:, t, ft * P:(ft + 1) * P], ident)
            ins.then_inc(x_turned, 1)

        def e_load(n, j, count, tiles, b0, per=2, extra=None):
            if n < E_Q + 4:
                pe.wait_ge(h_lo_ready, per * (j + 1))
            load(n, tiles, range(per * j, per * j + per), H, range(b0, b0 + count), j == 0, j == DT // per - 1, extra=extra)

        pe.wait_ge(x_ready, 4)
        for j in range(4):
            e_load(E_Q + j, j, 4, plain(512, 4), 0)
            if j == 1:
                pe.wait_ge(h_summed, 8)
                pe.wait_ge(x_ready, 8)
                mean(M_MIX0, 4, ones, acc[:, :])
        pe.wait_ge(rs_step, M_MIX0 + 1)
        e_load(E_KV, 0, 2, plain(256, 2), 4, 4)
        pe.wait_ge(gain_rows_loaded, 16 * GAIN_DMAS)
        pe.transpose(ps[:, 7, 0:N_GAINS], gain_rows[:, :], ident[0:N_GAINS, 0:N_GAINS]).then_inc(gains_turned, 1)
        e_load(E_KV + 1, 1, 2, plain(256, 2), 4, 4)
        pe.wait_ge(e_q_squared, 1)
        mean(M_EQ, 6, mean64, yb[:, 0, :])
        pe.wait_ge(gains_ready, 1)
        pe.wait_ge(e_q_squared, 2)
        mean(M_EQ + 1, 7, mean64, yb[:, 1, :])
        pe.wait_ge(e_q_scaled, 4)
        e_load(E_AIN, 0, 4, plain(512, 4), 0)
        pe.wait_ge(e_q_squared, 4)
        pe.wait_ge(rs_step, M_EQ + 1)
        mean(M_EQ + 2, 6, mean64, yb[:, 2, :])
        pe.wait_ge(rs_step, M_EQ + 2)
        mean(M_EQ + 3, 7, mean64, yb[:, 3, :])
        e_load(E_AIN + 1, 1, 4, plain(512, 4), 0)
        pe.wait_ge(e_k_squared, 1)
        pe.wait_ge(e_v_scaled, 1)
        mean(M_EK, 4, mean64, sq[:, 0, :])
        for t in range(QT):
            ins = pe.transpose(ps[:, 5, t * P:(t + 1) * P], e_vT[:, t * P:(t + 1) * P], ident)
        ins.then_inc(e_v_turned, 1)
        def e_scores(i):
            b0, k0 = 4, max(i - 1, 0)
            lo_ = 128 if i == 0 else 0
            if i:
                pe.wait_ge(a_biased, 4 * i)
            for h in (2, 3, 4, 5, 6, 7, 0, 1):
                if h == 0 and i >= 2:
                    pe.wait_ge(a_out, i - 1)
                a = 64 * (h // 4)
                c = 256 * (h % 2)
                ins = MM(ps[:, b0 + h // 2, c + lo_:c + 256], e_q[a:a + 64, h % 4, i * P:(i + 1) * P],
                         e_k[a:a + 64, k0 * P:(i + 1) * P], start=True, stop=True)
            ins.then_inc(a_scores, 1)

        def e_turn(i):
            pe.wait_ge(a_probs, HEADS * (i + 1))
            pe.wait_ge(a_biased, 4 * min(i + 2, QT))
            for kv in range(2):
                for part in ((1,) if i == 0 else (0, 1)):
                    for g in range(4):
                        ins = pe.transpose(ps[:, 4 + 2 * kv + part, g * P:(g + 1) * P],
                                           e_sc[:, i % 2, 4 * kv + g, part * P:(part + 1) * P], ident)
            ins.then_inc(a_probs_turned, 1)

        def e_values(i):
            if i:
                pe.wait_ge(a_pT_dve, 4 * i)
            else:
                pe.wait_ge(a_pT_act, 2)
            for kv in range(2):
                parts = (1,) if i == 0 else (0, 1)
                for part in parts:
                    ins = MM(ps[64 * kv:64 * kv + 64, 4, :], e_v[:, i - 1 + part, 64 * kv:64 * kv + 64],
                             e_pT[:, 2 * kv + part, :], start=part == parts[0], stop=part == 1)
            ins.then_inc(a_values, 1)

        ain = lambda j: e_load(E_AIN + j, j, 4, plain(512, 4), 0)
        ac = lambda j: e_load(E_AC + j, j, 4, plain(512, 4), 0)
        ab = lambda j, extra=None: e_load(E_AB + j, j, 4, plain(512, 4), 0, extra=extra)

        ain(2)
        pe.wait_ge(rs_used, 5)
        pe.wait_ge(e_v_ready, 1)
        e_scores(0)
        ain(3)
        e_scores(1)
        pe.wait_ge(conv_in_scaled, 4)
        ac(0)
        e_turn(0)
        ac(1)
        e_values(0)
        e_scores(2)
        ac(2)
        e_turn(1)
        ac(3)
        e_values(1)
        e_scores(3)
        pe.wait_ge(conv_h_ready, 4)
        ab(0)
        e_turn(2)
        ab(1, lambda: e_values(2))
        pe.wait_ge(a_out, 3)
        e_turn(3)
        ab(2, lambda: e_values(3))
        pe.wait_ge(yb_summed, 4)
        mean(M_EB, 5, ones, acc[:, :])
        ab(3)

        def out_group(n, b0, first2, last2, ready_sems, extra=None):
            for j in range(4):
                th, tl = first2 if j < 2 else last2
                pe.wait_ge(ready_sems[j // 2], 2 * (j % 2) + 2)
                load(n + j, plain(512, 4), range(2 * (j % 2), 2 * (j % 2) + 2), lambda k: (th[:, k, :], tl[:, k, :]),
                     range(b0, b0 + 4), j == 0, j == 3)
                if extra:
                    extra(j)

        def ea_mean(j):
            if j:
                return
            pe.wait_ge(ya_ready, 4)
            pe.wait_ge(ya_summed, 4)
            mean(M_EA, 0, ones, acc[:, :])

        pe.wait_ge(rs_step, M_EB + 1)
        out_group(E_OUT, 4, (yb_hi, yb_lo), (ya_hi, ya_lo), (yb_lo_ready, ya_lo_ready), ea_mean)
        pe.wait_ge(rs_step, M_EA + 1)
        out_group(E_OUT + 4, 0, (yb_hi, yb_lo), (ya_hi, ya_lo), (yb_lo_ready, ya_lo_ready))

        def ffn_in(layer, bank0):
            n0, n1, c = FFN_IN[layer], FFN_OUT[layer], 22 * layer
            rnd = 1 + 2 * layer

            def half_group(n, j, b0, shift):
                load(n + j, plain(256, 2), range(4 * (j // 2), 4 * (j // 2) + 4), H,
                     (b0 + 2 * (j % 2), b0 + 2 * (j % 2) + 1), j < 2, j >= 2, shift)

            pe.wait_ge(x_ready, 8 * rnd + 4)
            for j in range(4):
                if j in (0, 2):
                    pe.wait_ge(h_lo_ready, 8 * rnd + 2 * j + 4)
                half_group(n0, j, 4 * bank0, 0)
                if j == 1:
                    pe.wait_ge(x_ready, 8 * rnd + 8)
                    pe.wait_ge(h_summed, 8 * rnd + 8)
                    mean(M_FFN0 if layer == 0 else M_FFN1, (1 - bank0) * 4, ones, acc[:, :])
            pe.wait_ge(rs_step, (M_FFN0 if layer == 0 else M_FFN1) + 1)
            with pe.Fori(0, NG_FF // 2) as i:
                for g in (1, 2):
                    pe.wait_ge(hidden_ready, 1 + c + 2 * (g - 1) + 4 * i)
                    for j in range(4):
                        half_group(n0 + 4 * g, j, 4 * ((bank0 + g) % 2), 8 * i)

        def ffn_out(layer, bank0, half, extra=None):
            c = 22 * layer
            b0 = 4 * ((bank0 + 11 + half) % 2)
            m = FFN_OUT[layer] + 11 * half
            banks = range(b0, b0 + 4)
            A = lambda k: (act_hi[:, k, :], act_lo[:, k, :])
            pe.wait_ge(hidden_ready, 1 + c + 20 + 2 * half)
            pe.wait_ge(hidden_lo, c + 20)
            load(m, plain(512, 4), (0, 1), A, banks, True, False)
            if extra:
                extra()
            with pe.Fori(0, 2) as i:
                for j in range(1, 5):
                    ready(m + j, 4 * i)
                    wh, wl = w_hi[:, (m + j) % W_SLOTS, :], w_lo[:, (m + j) % W_SLOTS, :]
                    for kk in range(2):
                        k = bass.ds(8 * i + 2 * j + kk, 1)
                        mh = act_hi[:, k, :].rearrange("p k n -> p (k n)")
                        ml = act_lo[:, k, :].rearrange("p k n -> p (k n)")
                        for t in range(4):
                            st = slice(512 * kk + P * t, 512 * kk + P * t + P)
                            ins = product(ps[:, b0 + t, :], wh[:, st], wl[:, st], mh, ml, False, False)
                    ins.then_inc(load_used, 1)
            for j in (9, 10):
                if j == 10:
                    pe.wait_ge(hidden_lo, c + 22)
                load(m + j, plain(512, 4), (2 * j, 2 * j + 1), A, banks, False, j == 10)

        ffn_in(0, 1)
        ffn_out(0, 1, 0)
        ffn_out(0, 1, 1)

        pe.wait_ge(x_ready, 20)
        for j in range(4):
            pe.wait_ge(h_lo_ready, 16 + 2 * j + 2)
            load(O_CQ + j, plain(384, 3), (2 * j, 2 * j + 1), H, range(3), j == 0, j == 3)
            if j == 1:
                pe.wait_ge(x_ready, 24)
                pe.wait_ge(h_summed, 24)
                mean(M_MIX1, 4, ones, acc[:, :])
                for t in range(QT):
                    ins = MM(ps[:, 5, t:t + 1], acc[:, t * P:(t + 1) * P], ones[:, 0:1], start=True, stop=True)
                ins.then_inc(tok_sums, 1)
        pe.wait_ge(rs_step, M_MIX1 + 1)
        pe.wait_ge(tok_step, 1)
        for j in range(4):
            load(O_CKV + j, plain(512, 4), (2 * j, 2 * j + 1), H, range(4, 8), j == 0, j == 3)
            if j == 0:
                pe.wait_ge(cq_summed, 3)
                mean(M_CQ, 3, ones, acc[:, :])
        pe.wait_ge(rs_step, M_CQ + 1)
        pe.wait_ge(cq_scaled, 3)
        for j in range(4):
            n = O_CV + j
            ready(n)
            for kk in range(2):
                c = slice(512 * kk, 512 * kk + 512)
                for t in range(QT):
                    ins = product(ps[:, t, :], h_hi[:, 2 * j + kk, t * P:(t + 1) * P], h_lo[:, 2 * j + kk, t * P:(t + 1) * P],
                                  w_hi[:, n % W_SLOTS, c], w_lo[:, n % W_SLOTS, c], j == 0 and kk == 0, j == 3 and kk == 1)
            ins.then_inc(load_used, 1)
            if j == 0:
                pe.wait_ge(ckv_scaled, 4)
                pe.wait_ge(ckv_summed, 2)
                mean(M_CKV, 4, ones, acc[:, :])
                pe.wait_ge(ckv_squared, 3)
                mean(M_KR, 5, ones, sq[:, 0, :])
            if j == 1:
                pe.wait_ge(spatial_loaded, 32)
                for b in range(2):
                    for g in range(4):
                        ins = pe.transpose(ps[:, 6 + b, g * P:(g + 1) * P], w_sp[:, 4 * b + g, :], ident)
                    ins.then_inc(spatial_turned, 1)

        def q_load(j, b0):
            tiles = lambda w, kk: [w[:, 256 * kk + P * t:256 * kk + P * t + P] for t in range(2)]
            load(O_UQ + j, tiles, range(3), lambda k: (cq_hi[:, k, :], cq_lo[:, k, :]), (b0, b0 + 1), True, True)

        def q_means(hs, b0):
            for j, h in enumerate(hs):
                pe.wait_ge(oq_turned, h + 1)
                mean(M_OQ + h, b0 + j, mean_odd if h % 2 else mean_even, sq[:, h % 2, :])

        pe.wait_ge(cq_lo_ready, 3)
        pe.wait_ge(rs_step, M_KR + 1)
        pe.wait_ge(spatial_ready, 2)
        q_load(0, 4)
        q_load(1, 6)
        pe.wait_ge(cv_ready, 4)
        q_load(2, 0)
        q_means(range(4), 4)
        q_load(3, 2)

        def kv_load(half, b0):
            n = O_UKV + half
            ready(n)
            keys = lambda w, kk, j: w[:, n % W_SLOTS, 512 * kk + P * j:512 * kk + P * j + P]
            values = lambda w, kk: w[:, n % W_SLOTS, 512 * kk + 256:512 * kk + 512]
            for kk in range(2):
                for j in range(2):
                    product(ps[:, b0 + j, :], keys(w_hi, kk, j), keys(w_lo, kk, j),
                            ckv_hi[:, kk, :], ckv_lo[:, kk, :], kk == 0, kk == 1)
            for t in range(QT):
                for kk in range(2):
                    c = 256 * (t % 2)
                    ins = product(ps[:, b0 + 2 + t // 2, c:c + 256], ckv_hi[:, kk, t * P:(t + 1) * P],
                                  ckv_lo[:, kk, t * P:(t + 1) * P], values(w_hi, kk), values(w_lo, kk),
                                  kk == 0, kk == 1)
            ins.then_inc(load_used, 1)

        def k_means(half, b0):
            for j in range(2):
                pe.wait_ge(ok_gained, 2 * half + j + 1)
                mean(M_OK + 2 * half + j, b0 + j, mean64, sq[:, j, :])

        pe.wait_ge(ckv_lo_ready, 2)
        pe.wait_ge(rs_step, M_OQ + 4)
        kv_load(0, 4)
        q_means(range(4, 8), 0)
        pe.wait_ge(rs_step, M_OQ + 8)
        kv_load(1, 0)
        k_means(0, 4)
        pe.wait_ge(rs_step, M_OK + 2)
        pe.wait_ge(ov_act, 1)
        pe.wait_ge(ov_dve, 1)
        for j in range(4):
            load(O_CU + j, plain(512, 4), (2 * j, 2 * j + 1), H, range(4, 8), j == 0, j == 3)
            if j == 0:
                k_means(1, 0)
            if j == 1:
                pe.wait_ge(rs_step, M_OK + 4)
                pe.wait_ge(ov_act, 2)
                pe.wait_ge(ov_dve, 2)
                pe.wait_ge(cv_normed, 4)
                for g in range(8):
                    a = 64 * (g % 2)
                    for t in range(QT):
                        ins = MM(ps[a:a + 64, g // 2, t * P:(t + 1) * P], v_c[:, t, 64 * g:64 * g + 64], w_spT[:, g, :],
                                 start=True, stop=True)
                ins.then_inc(gates_mixed, 1)

        def o_scores(h):
            for n, i in enumerate(SCORE_ORDER):
                if h:
                    pe.wait_ge(d_exp_done, QT * (h - 1) + (1, 3, 3, 4)[n])
                s_ = score(i)
                MM(s_, o_q[:, h, i * P:(i + 1) * P], o_k[:, h, 0:P * (i + 1)], start=True, stop=False)
                MM(s_[:, P * i:P * (i + 1)], mask_q[:, :], mask_k[:, :], start=False, stop=True
                   ).then_inc(d_scores, 1)

        def o_turn(h):
            pe.wait_ge(d_probs, QT * (h + 1))
            if h:
                pe.wait_ge(d_pT_act, 2 * h)
                pe.wait_ge(d_pT_dve, h)
            for kt in range(QT):
                bank, c0 = ((4, 0), (5, 0), (6, 0), (5, 384))[kt]
                for i in range(kt, QT):
                    c = c0 + P * (i - kt)
                    ins = pe.transpose(ps[:, bank, c:c + P], o_p[:, h % 2, i, kt * P:(kt + 1) * P], ident)
            ins.then_inc(d_probs_turned, 1)

        def o_values(h):
            a = 64 * (h % 2)
            pe.wait_ge(d_pT_act, 2 * (h + 1))
            pe.wait_ge(d_pT_dve, h + 1)
            if h:
                pe.wait_ge(d_out, h)
            for kt in range(QT):
                pT = (o_pT[:, 0, :], o_pT[:, 1, 0:384], o_pT[:, 2, 0:256], o_pT[:, 1, 384:512])[kt]
                ins = MM(ps[a:a + 64, 7, P * kt:S], o_v[:, kt, 64 * h:64 * h + 64], pT,
                         start=kt == 0, stop=kt == QT - 1)
            ins.then_inc(d_values, 1)

        pe.wait_ge(gates_ready, 4)
        pe.wait_ge(rs_used, 22)
        pe.wait_ge(kr_copied, HEADS)
        pe.wait_ge(columns_set, 1)
        o_scores(0)
        pe.wait_ge(yc_summed, 4)
        mean(M_OC, 3, ones, acc[:, :])
        pe.wait_ge(u_scaled, 4)
        for h in range(HEADS):
            if h + 1 < HEADS:
                o_scores(h + 1)
            if h:
                o_values(h - 1)
            o_turn(h)

        def od_mean(j):
            if j == 0:
                o_values(7)
            if j == 1:
                pe.wait_ge(yd_summed, 4)
                mean(M_OD, 4, ones, acc[:, :])

        pe.wait_ge(rs_step, M_OC + 1)
        out_group(O_OUT, 0, (yc_hi, yc_lo), (yd_hi, yd_lo), (yc_lo_ready, yd_lo_ready), od_mean)
        pe.wait_ge(rs_step, M_OD + 1)
        out_group(O_OUT + 4, 4, (yc_hi, yc_lo), (yd_hi, yd_lo), (yc_lo_ready, yd_lo_ready))
        ffn_in(1, 0)

        def turn_out(half, b0):
            pe.wait_ge(x_ready, 32 + 4 * half + 4)
            for t in range(QT):
                for j in range(4):
                    ins = pe.transpose(ps[:, b0 + t, j * P:(j + 1) * P], xT[:, 4 * half + j, t * P:(t + 1) * P], ident)
                ins.then_inc(out_turned, 1)

        ffn_out(1, 0, 0)
        ffn_out(1, 0, 1, lambda: turn_out(0, 4))
        turn_out(1, 0)
    ctx.close()


_INS = ["x", "mix_norm", "ffn_norm", "w_ffn_in", "w_ffn_out", "e_w_in", "e_conv", "e_q_gain", "e_k_gain",
        "e_sinks", "e_out_gain", "e_w_out", "o_w_in", "o_spatial", "o_spatial_bias", "o_v_gain",
        "o_q_a_gain", "o_kv_a_gain", "o_w_uq", "o_w_ukv", "o_q_gain", "o_k_gain", "o_out_gain", "o_w_out"]


def constants():
    f = np.float32
    blk = np.zeros((3, P, P), f)
    for a in (0, 64):
        blk[0, a:a + 64, a:a + 64] = 1 / 64
    blk[1, 0:64, 0:64] = 1 / 64
    blk[1, 64:96, 64:128] = 1 / 32
    blk[2, 64:128, 64:128] = 1 / 64
    blk[2, 0:32, 0:64] = 1 / 32
    small = np.concatenate([np.eye(P, dtype=f), np.ones((P, P), f), blk[0], blk[1], blk[2]], axis=1)
    pos = np.arange(S, dtype=f)
    inv = (f(10000.0) ** (-np.arange(0, 32, 2, dtype=f) / f(32))).astype(f)
    ang = (pos[None, :] * inv[:, None]).astype(f)
    cos = np.concatenate([np.cos(ang)] * 2)
    sin = np.concatenate([-np.sin(ang), np.sin(ang)])
    one = np.ones((64, S), f)
    tables = np.concatenate([np.tile(cos, (4, 1)), np.tile(sin, (4, 1)),
                             np.concatenate([one, cos, sin]), np.concatenate([cos, sin, one])], axis=1)
    q, k = np.arange(P)[:, None], np.arange(256)[None, :] - P
    seen = (k // 64 <= q // 64) & (k // 64 >= q // 64 - 1)
    slopes = 2.0 ** -np.arange(1, HEADS + 1)
    alibi = np.where(seen[:, None, :], -slopes[None, :, None] * np.abs(q - k)[:, None, :], NEG)
    return small.astype(f), tables.astype(f), alibi.reshape(P, HEADS * 256).astype(f)


def kernel(**inputs):
    import concourse.bacc as bacc
    from concourse.bass_utils import run_bass_kernel_spmd as run

    nc = bacc.Bacc("TRN2", target_bir_lowering=False, num_devices=1)
    arrays, args = {}, []
    for name in _INS:
        a = np.ascontiguousarray(inputs[name])
        arrays[f"in_{name}"] = a
        args.append(nc.dram_tensor(f"in_{name}", a.shape, mybir.dt.from_np(a.dtype), kind="ExternalInput").ap())
    for name, a in zip(("small", "tables", "alibi"), constants()):
        a = np.ascontiguousarray(a)
        arrays[f"const_{name}"] = a
        args.append(nc.dram_tensor(f"const_{name}", a.shape, F32, kind="ExternalInput").ap())
    args.append(nc.dram_tensor("out_0_dram", (1, S, D), F32, kind="ExternalOutput").ap())
    program(nc, *args)
    r = run(nc, [arrays], core_ids=[0])
    return r.results[0]["out_0_dram"]
```

```python
from contextlib import ExitStack

import numpy as np
import concourse.bass as bass
from concourse import mybir

F32 = mybir.dt.float32
F32R = mybir.dt.float32r
BF16 = mybir.dt.bfloat16

ACT = mybir.ActivationFunctionType
ALU = mybir.AluOpType
AX = mybir.AxisListType.X

P = 128
S = 512
D = 1024
DT = D // P
FF = 2816
FT = FF // P
NG_FF = FF // 256
EPS = 1e-6
HEADS = 8
QT = S // P
E_SCALE = 64 ** -0.5
O_SCALE = 96 ** -0.5
NEG = -1e30

RAW_SLOTS = 2
W_SLOTS = 4
LEAD = W_SLOTS

E_Q, E_KV, E_AIN, E_AC, E_AB, E_OUT = 0, 4, 6, 10, 14, 18
FFN_IN = (26, 122)
FFN_OUT = (70, 166)
O_CQ, O_CKV, O_CV, O_UKV, O_OUT = 92, 96, 100, 112, 114
O_UQ, O_CU = (104, 105, 108, 109), (106, 107, 110, 111)
N_LOADS = 188

(M_MIX0, M_EQ, M_EK, M_EB, M_EA, M_FFN0, M_MIX1, M_CQ, M_CKV, M_KR, M_OQ, M_OK, M_OC, M_OD,
 M_FFN1) = (0, 1, 5, 6, 7, 8, 9, 10, 11, 12, 13, 21, 25, 26, 27)
TO_ROW_SCALE = (M_MIX0, M_FFN0, M_MIX1, M_FFN1)

G_FFN0, G_MIX1, G_FFN1, G_EA, G_EB, G_CONV, G_OOUT = 0, 8, 16, 24, 28, 32, 44
G_CQ, G_CKV, G_V, G_EQ, G_EK, G_OQE, G_OQO, G_OK, G_KR = 52, 55, 57, 61, 62, 63, 64, 65, 66
N_GAINS = 67
N_SMALL = 768
TAB_KEY, TAB_EVEN, TAB_ODD = 0, 512, 1024


def load_width(n):
    if O_CQ <= n < O_CV:
        return 768
    if n in O_UQ:
        return 768
    return 1024


def ordered(n, split, source):
    if E_Q <= n < E_KV:
        if source is not None:
            return [source[:, 512 * k:512 * k + 512].rearrange("p (g j c) -> p g j c", g=2, j=4) for k in range(2)]
        return [split[:, 512 * k:512 * k + 512].rearrange("p (j g c) -> p g j c", g=2, j=4) for k in range(2)]
    if O_UKV <= n < O_OUT:
        if source is not None:
            return [source[:, 512 * k:512 * k + 512].rearrange("p (h two c) -> p h two c", h=4, two=2) for k in range(2)]
        return [split[:, 512 * k:512 * k + 512].rearrange("p (two h c) -> p h two c", h=4, two=2) for k in range(2)]
    w = load_width(n)
    return [(split if source is None else source)[:, 0:w]]


def load_dmas(n):
    if E_Q <= n < E_KV:
        return 1
    if n in (E_OUT, E_OUT + 1, E_OUT + 4, E_OUT + 5):
        return 2
    if n in O_UQ:
        return 3
    return 1


def landed(n):
    return 16 * sum(load_dmas(m) for m in range(n % RAW_SLOTS, n + 1, RAW_SLOTS))


GAIN_DMAS = 10 + 6 + 3 + 4 + 6


def program(nc, x, mix_norm, ffn_norm, w_ffn_in, w_ffn_out, e_w_in, e_conv, e_q_gain, e_k_gain,
            e_sinks, e_out_gain, e_w_out, o_w_in, o_spatial, o_spatial_bias, o_v_gain,
            o_q_a_gain, o_kv_a_gain, o_w_uq, o_w_ukv, o_q_gain, o_k_gain, o_out_gain, o_w_out,
            c_small, c_tables, c_alibi, out):
    ctx = ExitStack()
    base = (nc.sbuf_base + 31) // 32 * 32
    top = nc.sbuf_top
    place = [base]

    def at(name, shape, dt, offset):
        return nc.alloc_sbuf_tensor_at(name, shape, dt, offset=offset)

    def sb(name, shape, dt=F32, size=4):
        n = size
        for d in shape[1:]:
            n *= d
        t = at(name, shape, dt, place[0])
        place[0] += (n + 31) // 32 * 32
        return t

    xT = sb("xT", [P, DT, S])
    h_at = place[0]
    h_hi = sb("h_hi", [P, DT, S], F32R)
    h_lo = sb("h_lo", [P, DT, S], F32R)
    out_tok = at("out_tok", [P, QT, D], F32, h_at)
    raw = sb("raw", [P, RAW_SLOTS, 1024])
    w_hi = sb("w_hi", [P, W_SLOTS, 1024], F32R)
    w_lo = sb("w_lo", [P, W_SLOTS, 1024], F32R)
    small = sb("small", [P, N_SMALL])
    ident, ones = small[:, 0:128], small[:, 128:256]
    mean64, mean_even, mean_odd, turn = (small[:, P * i:P * i + P] for i in (2, 3, 4, 5))
    tables = sb("tables", [P, 3 * S])
    gains = sb("gains", [P, N_GAINS])
    mix0_gain = sb("mix0_gain", [P, DT])
    gate_bias = sb("gate_bias", [P, 4, P])
    sinks = sb("sinks", [P, HEADS])
    eps_col = sb("eps_col", [P, 1])
    spare = sb("spare", [P, 1])
    mask_q = sb("mask_q", [1, P], BF16, 2)
    mask_k = sb("mask_k", [1, P], BF16, 2)
    tiny = sb("tiny", [P, 16, 8])
    row_scale = sb("row_scale", [P, S])
    acc = sb("acc", [P, S])
    temp_at = place[0]
    sq = sb("sq", [P, 2, S])
    y0 = sb("y0", [P, 2, S])
    rs = sb("rs", [P, 2, S])
    ffn_t = at("ffn_t", [P, 4, S], F32, temp_at)
    R = place[0]
    K = 1024
    act_hi = at("act_hi", [P, FT, S], F32R, R)
    act_lo = at("act_lo", [P, FT, S], F32R, R + FT * S * 4)
    assert R + 2 * FT * S * 4 <= top, (R + 2 * FT * S * 4, top)
    x_tok = at("x_tok", [P, QT, D], F32, R)
    e_sc = at("e_sc", [P, 2, HEADS, 256], F32, R)
    yb_hi = at("yb_hi", [P, 4, S], F32R, R)
    yb_lo = at("yb_lo", [P, 4, S], F32R, R + 8 * K)
    alibi = at("alibi", [P, HEADS, 256], F32, R + 16 * K)
    e_pT = at("e_pT", [P, 4, S], F32, R + 24 * K)
    e_q = at("e_q", [P, 4, S], F32, R + 32 * K)
    e_k = at("e_k", [P, S], F32, R + 40 * K)
    e_vT = at("e_vT", [P, S], F32, R + 42 * K)
    e_v = at("e_v", [P, QT, P], F32, R + 44 * K)
    conv_h = at("conv_h", [P, 4, S], F32, R + 46 * K)
    conv_y = at("conv_y", [P, 4, S], F32, R + 54 * K)
    yb = at("yb", [P, 4, S], F32, R + 62 * K)
    ya_hi = at("ya_hi", [P, 4, S], F32R, R + 70 * K)
    ya_lo = at("ya_lo", [P, 4, S], F32R, R + 78 * K)
    gain_rows = at("gain_rows", [N_GAINS, P], F32, R + 86 * K)
    o_q = at("o_q", [P, HEADS, S], F32, R)
    yd_hi = at("yd_hi", [P, 4, S], F32R, R)
    yd_lo = at("yd_lo", [P, 4, S], F32R, R + 8 * K)
    o_k = at("o_k", [P, HEADS, S], F32, R + 16 * K)
    o_v = at("o_v", [P, QT, S], F32, R + 32 * K)
    o_p = at("o_p", [P, 2, 1280], F32, R + 40 * K)
    cq = at("cq", [P, 3, S], F32, R + 40 * K)
    k_pairs = (at("k_pair_a", [P, 2, S], F32, R + 45 * K), at("k_pair_b", [P, 2, S], F32, R + 72 * K))
    sq_more = at("sq_more", [P, 2, S], F32, R + 48 * K)
    u_c = at("u_c", [P, 4, S], F32, R + 60 * K)
    w_sp = at("w_sp", [P, HEADS, P], F32, R + 48 * K)
    kr = at("kr", [P, 2, S], F32, R + 52 * K)
    yc = at("yc", [P, 4, S], F32, R + 50 * K)
    o_pT = at("o_pT", [P, 3, S], F32, R + 58 * K)
    cq_hi = at("cq_hi", [P, 3, S], F32R, R + 56 * K)
    cq_lo = at("cq_lo", [P, 3, S], F32R, R + 62 * K)
    ckv = at("ckv", [P, 2, S], F32, R + 68 * K)
    w_spT = at("w_spT", [P, HEADS, P], F32, R + 68 * K)
    yd = at("yd", [P, 4, S], F32, R + 64 * K)
    v_c = at("v_c", [P, QT, S], F32, R + 72 * K)
    ckv_hi = at("ckv_hi", [P, 2, S], F32R, R + 80 * K)
    ckv_lo = at("ckv_lo", [P, 2, S], F32R, R + 84 * K)
    yc_hi = at("yc_hi", [P, 4, S], F32R, R + 72 * K)
    yc_lo = at("yc_lo", [P, 4, S], F32R, R + 80 * K)

    ps = ctx.enter_context(nc.psum_tensor("ps", [P, 8, S], F32))

    def sem(name):
        return ctx.enter_context(nc.semaphore(name))

    raw_landed = [sem(f"raw_landed{i}") for i in range(RAW_SLOTS)]
    hi_done = sem("hi_done")
    lo_done = sem("lo_done")
    load_used = sem("load_used")
    small_loaded = sem("small_loaded")
    means_loaded = sem("means_loaded")
    x_loaded = [sem(f"x_loaded{i}") for i in range(4)]
    mix0_loaded = sem("mix0_loaded")
    tables_loaded = sem("tables_loaded")
    alibi_loaded = sem("alibi_loaded")
    gain_rows_loaded = sem("gain_rows_loaded")
    sinks_loaded = sem("sinks_loaded")
    gate_bias_loaded = sem("gate_bias_loaded")
    columns_set = sem("columns_set")
    spatial_loaded = sem("spatial_loaded")
    spatial_zeroed = sem("spatial_zeroed")
    x_turned = sem("x_turned")
    x_ready = sem("x_ready")
    h_hi_ready = sem("h_hi_ready")
    h_squared = sem("h_squared")
    h_lo_ready = sem("h_lo_ready")
    h_summed = sem("h_summed")
    gains_turned = sem("gains_turned")
    gains_ready = sem("gains_ready")
    sums_ready = sem("sums_ready")
    rs_first = sem("rs_first")
    rs_square = sem("rs_square")
    rs_step = sem("rs_step")
    rs_ready = sem("rs_ready")
    rs_used = sem("rs_used")
    e_q_scaled = sem("e_q_scaled")
    e_q_squared = sem("e_q_squared")
    e_k_scaled = sem("e_k_scaled")
    e_k_squared = sem("e_k_squared")
    e_v_scaled = sem("e_v_scaled")
    e_v_turned = sem("e_v_turned")
    e_v_ready = sem("e_v_ready")
    conv_in_scaled = sem("conv_in_scaled")
    conv_in_ready = sem("conv_in_ready")
    conv_h_ready = sem("conv_h_ready")
    conv_tap_a = sem("conv_tap_a")
    conv_tap_b = sem("conv_tap_b")
    conv_tap_c = sem("conv_tap_c")
    conv_y_scaled = sem("conv_y_scaled")
    a_scores = sem("a_scores")
    a_biased = sem("a_biased")
    a_row_max = sem("a_row_max")
    a_max = sem("a_max")
    a_neg_max = sem("a_neg_max")
    a_sink_diff = sem("a_sink_diff")
    a_exp_done = sem("a_exp_done")
    a_sink_exp = sem("a_sink_exp")
    a_denominator = sem("a_denominator")
    a_inverse = sem("a_inverse")
    a_probs = sem("a_probs")
    a_probs_turned = sem("a_probs_turned")
    a_pT_act = sem("a_pT_act")
    a_pT_dve = sem("a_pT_dve")
    a_values = sem("a_values")
    a_out = sem("a_out")
    yb_squared = sem("yb_squared")
    yb_summed = sem("yb_summed")
    yb_normed = sem("yb_normed")
    yb_hi_ready = sem("yb_hi_ready")
    yb_lo_ready = sem("yb_lo_ready")
    ya_ready = sem("ya_ready")
    ya_squared = sem("ya_squared")
    ya_summed = sem("ya_summed")
    ya_normed = sem("ya_normed")
    ya_hi_ready = sem("ya_hi_ready")
    ya_lo_ready = sem("ya_lo_ready")
    gate_scaled = sem("gate_scaled")
    silu_done = sem("silu_done")
    silu_scaled = sem("silu_scaled")
    hidden_ready = sem("hidden_ready")
    hidden_hi = sem("hidden_hi")
    hidden_lo = sem("hidden_lo")
    tok_sums = sem("tok_sums")
    tok_first = sem("tok_first")
    tok_square = sem("tok_square")
    tok_step = sem("tok_step")
    tok_scale = sem("tok_scale")
    cq_scaled = sem("cq_scaled")
    cq_squared = sem("cq_squared")
    cq_summed = sem("cq_summed")
    cq_normed = sem("cq_normed")
    cq_hi_ready = sem("cq_hi_ready")
    cq_lo_ready = sem("cq_lo_ready")
    ckv_scaled = sem("ckv_scaled")
    ckv_squared = sem("ckv_squared")
    ckv_summed = sem("ckv_summed")
    ckv_normed = sem("ckv_normed")
    ckv_hi_ready = sem("ckv_hi_ready")
    ckv_lo_ready = sem("ckv_lo_ready")
    kr_normed = sem("kr_normed")
    kr_terms = sem("kr_terms")
    kr_added = sem("kr_added")
    kr_rotated = sem("kr_rotated")
    kr_copied = sem("kr_copied")
    kr_columns = sem("kr_columns")
    uq_columns = sem("uq_columns")
    spatial_turned = sem("spatial_turned")
    spatial_ready = sem("spatial_ready")
    cv_ready = sem("cv_ready")
    cv_squared = sem("cv_squared")
    cv_first = sem("cv_first")
    cv_square = sem("cv_square")
    cv_step = sem("cv_step")
    cv_scale = sem("cv_scale")
    cv_normed = sem("cv_normed")
    oq_squared = sem("oq_squared")
    oq_turned = sem("oq_turned")
    ok_squared = sem("ok_squared")
    ok_gained = sem("ok_gained")
    ok_normed = sem("ok_normed")
    ov_act = sem("ov_act")
    ov_dve = sem("ov_dve")
    gates_mixed = sem("gates_mixed")
    gates_ready = sem("gates_ready")
    u_scaled = sem("u_scaled")
    u_ready = sem("u_ready")
    yc_ready = sem("yc_ready")
    yc_squared = sem("yc_squared")
    yc_summed = sem("yc_summed")
    yc_normed = sem("yc_normed")
    yc_hi_ready = sem("yc_hi_ready")
    yc_lo_ready = sem("yc_lo_ready")
    d_scores = sem("d_scores")
    d_neg_max = sem("d_neg_max")
    d_exp_done = sem("d_exp_done")
    d_inverse = sem("d_inverse")
    d_probs = sem("d_probs")
    d_probs_turned = sem("d_probs_turned")
    d_pT_act = sem("d_pT_act")
    d_pT_dve = sem("d_pT_dve")
    d_values = sem("d_values")
    d_out = sem("d_out")
    yd_squared = sem("yd_squared")
    yd_summed = sem("yd_summed")
    yd_normed = sem("yd_normed")
    yd_hi_ready = sem("yd_hi_ready")
    yd_lo_ready = sem("yd_lo_ready")
    out_turned = sem("out_turned")
    out_act = sem("out_act")
    out_dve = sem("out_dve")
    out_stored = sem("out_stored")

    def used_before(m):
        return sum(1 for i in range(m + 1) if i not in TO_ROW_SCALE)

    block = ctx.enter_context(nc.Block())

    def x_quarter(queue, i):
        c = slice(256 * i, 256 * i + 256)
        queue.dma_start(x_tok[:, :, c], x[0].rearrange("(t p) c -> p t c", p=P)[:, :, c]).then_inc(x_loaded[i], 16)

    @block.sync
    def _(sp):
        sp.dma_start(small[:, 0:256], c_small[:, 0:256]).then_inc(small_loaded, 16)
        x_quarter(sp, 0)

        def free(n):
            if n >= RAW_SLOTS:
                sp.wait_ge(lo_done, n - RAW_SLOTS + 1)

        def wide(n, w, rows, c0, cols):
            free(n)
            dst = raw[:, n % 2, 0:2 * cols].rearrange("p (k n) -> p k n", k=2)
            src = w[rows:rows + 256, c0:c0 + cols].rearrange("(k p) n -> p k n", p=P)
            sp.dma_start(dst, src).then_inc(raw_landed[n % 2], 16)

        ein = e_w_in[0]
        for j in range(4):
            wide(E_Q + j, ein, 256 * j, 1536, 512)
            if j == 0:
                x_quarter(sp, 2)
            if j == 1:
                sp.dma_start(small[:, 256:], c_small[:, 256:]).then_inc(means_loaded, 16)
        for j in range(2):
            n = E_KV + j
            free(n)
            sp.dma_start(raw[:, n % 2, :].rearrange("p (k n) -> p k n", k=4),
                         ein[512 * j:512 * j + 512, 2048:2304].rearrange("(k p) n -> p k n", p=P)
                         ).then_inc(raw_landed[n % 2], 16)
        sp.dma_start(alibi[:, :, :], c_alibi.rearrange("p (h k) -> p h k", h=HEADS)).then_inc(alibi_loaded, 16)
        sp.dma_start(tables[:, :], c_tables).then_inc(tables_loaded, 16)
        for s0, c0 in ((E_AIN, 0), (E_AC, 1024), (E_AB, 512)):
            for j in range(4):
                wide(s0 + j, ein, 256 * j, c0, 512)
        for half in range(2):
            for j in range(2):
                n = E_OUT + 4 * half + j
                free(n)
                for g in range(2):
                    r0 = 512 + 256 * g + 128 * j
                    sp.dma_start(raw[64 * g:64 * g + 64, n % 2, :].rearrange("p (k n) -> p k n", k=2),
                                 e_w_out[0, r0:r0 + 128, 512 * half:512 * half + 512]
                                 .rearrange("(k p) n -> p k n", p=64)).then_inc(raw_landed[n % 2], 16)
            for j in range(2):
                wide(E_OUT + 4 * half + 2 + j, e_w_out[0], 256 * j, 512 * half, 512)

        def ffn(layer):
            n0 = FFN_IN[layer]
            w = w_ffn_in[layer].rearrange("(k p) n -> p k n", p=P)
            with sp.Fori(0, NG_FF) as g:
                for j in range(4):
                    kh, two = j // 2, j % 2
                    sp.wait_ge(lo_done, n0 + j - 1 + 4 * g)
                    sp.dma_start(raw[:, (n0 + j) % 2, :].rearrange("p (k n) -> p k n", k=4),
                                 w[:, 4 * kh:4 * kh + 4, bass.ds(FF * two + g * 256, 256)]
                                 ).then_inc(raw_landed[(n0 + j) % 2], 16)
            n1 = FFN_OUT[layer]
            w = w_ffn_out[layer].rearrange("(k p) n -> p k n", p=P)
            for half in range(2):
                with sp.Fori(0, 5) as i:
                    for j in range(2):
                        n = n1 + 11 * half + j
                        sp.wait_ge(lo_done, n - 1 + 2 * i)
                        sp.dma_start(raw[:, n % 2, :].rearrange("p (k n) -> p k n", k=2),
                                     w[:, bass.ds(4 * i + 2 * j, 2), 512 * half:512 * half + 512]
                                     ).then_inc(raw_landed[n % 2], 16)
                wide(n1 + 11 * half + 10, w_ffn_out[layer], 20 * P, 512 * half, 512)

        ffn(0)
        oin = o_w_in[0]
        for j in range(4):
            wide(O_CQ + j, oin, 256 * j, 1024, 384)
        for j in range(4):
            n = O_CKV + j
            free(n)
            sp.dma_start(raw[:, n % 2, 0:768].rearrange("p (k n) -> p k n", k=2)[:, :, 0:288],
                         oin[256 * j:256 * j + 256, 1408:1696].rearrange("(k p) n -> p k n", p=P)
                         ).then_inc(raw_landed[n % 2], 16)
        sp.wait_ge(load_used, FFN_OUT[0] + 22)
        sp.wait_ge(spatial_zeroed, 1)
        ws = o_spatial[0].rearrange("g i j -> i g j")
        sp.dma_start(w_sp[0:64, :, 0:64], ws[0:64, :, 0:64]).then_inc(spatial_loaded, 16)
        sp.dma_start(w_sp[64:128, :, :], ws[64:128, :, :]).then_inc(spatial_loaded, 16)
        for j in range(4):
            wide(O_CV + j, oin, 256 * j, 512, 512)
        for n in range(O_UQ[0], O_UKV):
            if n in O_CU:
                wide(n, oin, 256 * O_CU.index(n), 0, 512)
                continue
            j = O_UQ.index(n)
            free(n)
            dst = raw[:, n % 2, 0:768].rearrange("p (k n) -> p k n", k=3)
            src = o_w_uq[0].rearrange("(k p) n -> p k n", p=P)
            he, ho = 96 * 2 * j, 96 * (2 * j + 1)
            sp.dma_start(dst[:, :, 0:96], src[:, :, he:he + 96]).then_inc(raw_landed[n % 2], 16)
            sp.dma_start(dst[:, :, 128:160], src[:, :, ho + 64:ho + 96]).then_inc(raw_landed[n % 2], 16)
            sp.dma_start(dst[:, :, 192:256], src[:, :, ho:ho + 64]).then_inc(raw_landed[n % 2], 16)
        for j in range(2):
            wide(O_UKV + j, o_w_ukv[0], 0, 512 * j, 512)
        for half in range(2):
            for j in range(4):
                wide(O_OUT + 4 * half + j, o_w_out[0], 256 * j, 512 * half, 512)
        ffn(1)
        for half in range(2):
            for t in range(QT):
                sp.wait_ge((out_act, out_dve)[t % 2], 2 * half + t // 2 + 1)
                sp.dma_start(out[0, t * P:(t + 1) * P, 512 * half:512 * half + 512],
                             out_tok[:, t, 512 * half:512 * half + 512]).then_inc(out_stored, 16)
        sp.wait_ge(out_stored, 16 * 8)

    @block.gpsimd
    def _(pool):
        rows = gain_rows
        pool.memset(eps_col[:, :], EPS)
        pool.memset(mask_q[:, 0:64], 1.0)
        pool.memset(mask_q[:, 64:128], 0.0)
        pool.memset(mask_k[:, 0:64], 0.0)
        pool.memset(mask_k[:, 64:128], NEG).then_inc(columns_set, 1)
        n_gain = [0]

        def row(dst, src):
            pool.dma_start(dst, src).then_inc(gain_rows_loaded, 16)
            n_gain[0] += 1

        row(rows[G_FFN0:G_FFN0 + 8, :], ffn_norm[0].rearrange("(r c) -> r c", c=P))
        row(rows[G_MIX1:G_MIX1 + 8, :], mix_norm[1].rearrange("(r c) -> r c", c=P))
        row(rows[G_FFN1:G_FFN1 + 8, :], ffn_norm[1].rearrange("(r c) -> r c", c=P))
        row(rows[G_EA:G_EA + 4, :], e_out_gain[0, 0:512].rearrange("(r c) -> r c", c=P))
        row(rows[G_EB:G_EB + 4, :].rearrange("r (g c) -> r g c", g=2),
            e_out_gain[0, 512:1024].rearrange("(g r c) -> r g c", g=2, c=64))
        row(rows[G_CONV:G_CONV + 12, :], e_conv[0].rearrange("t (r c) -> (t r) c", c=P))
        row(rows[G_OOUT:G_OOUT + 8, :], o_out_gain[0].rearrange("(r c) -> r c", c=P))
        row(rows[G_CQ:G_CQ + 3, :], o_q_a_gain[0].rearrange("(r c) -> r c", c=P))
        row(rows[G_CKV:G_CKV + 2, :], o_kv_a_gain[0].rearrange("(r c) -> r c", c=P))
        row(rows[G_V:G_V + 4, :], o_v_gain[0].rearrange("(r c) -> r c", c=P))
        for r, g in ((G_EQ, e_q_gain), (G_EK, e_k_gain), (G_OK, o_k_gain)):
            for i in range(2):
                row(rows[r:r + 1, 64 * i:64 * i + 64], g[0:1, 0:64])
        row(rows[G_OQE:G_OQE + 1, 0:96], o_q_gain[0:1, 0:96])
        row(rows[G_OQE:G_OQE + 1, 96:112], o_q_gain[0:1, 80:96])
        row(rows[G_OQE:G_OQE + 1, 112:128], o_q_gain[0:1, 64:80])
        row(rows[G_OQO:G_OQO + 1, 0:32], o_q_gain[0:1, 64:96])
        row(rows[G_OQO:G_OQO + 1, 32:48], o_q_gain[0:1, 80:96])
        row(rows[G_OQO:G_OQO + 1, 48:64], o_q_gain[0:1, 64:80])
        row(rows[G_OQO:G_OQO + 1, 64:128], o_q_gain[0:1, 0:64])
        for i in range(2):
            row(rows[G_KR:G_KR + 1, 64 * i:64 * i + 32], o_k_gain[0:1, 64:96])
            row(rows[G_KR:G_KR + 1, 64 * i + 32:64 * i + 48], o_k_gain[0:1, 80:96])
            row(rows[G_KR:G_KR + 1, 64 * i + 48:64 * i + 64], o_k_gain[0:1, 64:80])
        assert n_gain[0] == GAIN_DMAS
        pool.dma_start(sinks[:, :], e_sinks[0:1, :].broadcast_to([P, HEADS])).then_inc(sinks_loaded, 16)
        for g in range(2):
            pool.dma_start(gate_bias[64 * g:64 * g + 64, :, :],
                           o_spatial_bias.rearrange("a (j g) i -> a g j i", g=2)[:, g]
                           .broadcast_to([64, 4, P])).then_inc(gate_bias_loaded, 16)

        for j in range(4):
            pool.wait_ge(conv_in_scaled, j + 1)
            pool.tensor_tensor(conv_h[:, j, :], conv_h[:, j, :], row_scale[:, :], ALU.mult).then_inc(conv_in_ready, 1)
        for j in range(4):
            pool.wait_ge(conv_tap_c, j + 1)
            pool.tensor_tensor(conv_y[:, j, :], conv_y[:, j, :], row_scale[:, :], ALU.mult).then_inc(conv_y_scaled, 1)

        def scale_silus(layer):
            with pool.Fori(0, NG_FF // 2) as i:
                for t in range(4):
                    pool.wait_ge(silu_done, 22 * layer + t + 1 + 4 * i)
                    pool.tensor_tensor(ffn_t[:, t, :], ffn_t[:, t, :], row_scale[:, :], ALU.mult).then_inc(silu_scaled, 1)
            for t in range(2):
                pool.wait_ge(silu_done, 22 * layer + 20 + t + 1)
                pool.tensor_tensor(ffn_t[:, t, :], ffn_t[:, t, :], row_scale[:, :], ALU.mult).then_inc(silu_scaled, 1)

        scale_silus(0)
        pool.wait_ge(load_used, FFN_OUT[0] + 22)
        pool.memset(w_sp[0:64, :, 64:128], 0.0).then_inc(spatial_zeroed, 1)
        for j in range(4):
            n = O_CKV + j
            pool.wait_ge(raw_landed[n % 2], landed(n))
            v = raw[:, n % 2, 0:768].rearrange("p (k n) -> p k n", k=2)
            for k in range(2):
                one = v[:, k, 256:288].unsqueeze(1)
                pool.tensor_copy(v[:, k, 320:352], v[:, k, 256:288])
                both = v[:, k, 256:384].rearrange("p (r c) -> p r c", r=2)
                pool.tensor_copy(both[:, :, 32:48], one[:, :, 16:32].broadcast_to([P, 2, 16]))
                ins = pool.tensor_copy(both[:, :, 48:64], one[:, :, 0:16].broadcast_to([P, 2, 16]))
            ins.then_inc(kr_columns, 1)
        def uq_swap(j):
            n = O_UQ[j]
            pool.wait_ge(raw_landed[n % 2], landed(n))
            v = raw[:, n % 2, 0:768].rearrange("p (k n) -> p k n", k=3)
            for o in (64, 128):
                pool.tensor_copy(v[:, :, o + 32:o + 48], v[:, :, o + 16:o + 32])
                ins = pool.tensor_copy(v[:, :, o + 48:o + 64], v[:, :, o:o + 16])
            ins.then_inc(uq_columns, 1)

        uq_swap(0)
        uq_swap(1)
        pool.wait_ge(kr_rotated, 1)
        pool.wait_ge(uq_columns, 2)
        for n, h in enumerate((0, 2, 4, 6, 1, 3, 5, 7)):
            a = 64 * (1 - h % 2)
            if n == 4:
                pool.wait_ge(kr_copied, 4)
            pool.tensor_copy(o_k[a:a + 64, h, :], kr[a:a + 64, 1, :]).then_inc(kr_copied, 1)
        pool.wait_ge(kr_copied, HEADS)
        uq_swap(2)
        uq_swap(3)
        for h in range(HEADS):
            m = M_OQ + h
            pool.wait_ge(rs_ready, m + 1)
            pool.tensor_tensor(o_q[:, h, :], o_q[:, h, :], rs[:, m % 2, :], ALU.mult).then_inc(rs_used, 1)
        pool.wait_ge(rs_used, used_before(M_OQ + 7))
        for p in range(4):
            m = M_OK + p
            pool.wait_ge(rs_ready, m + 1)
            pool.wait_ge(ok_normed, p + 1)
            pool.tensor_tensor(o_k[64:128, 2 * p + 1, :], k_pairs[p // 2][64:128, p % 2, :], rs[64:128, m % 2, :], ALU.mult
                               ).then_inc(rs_used, 1)
        pool.wait_ge(rs_used, used_before(M_OK + 3))
        scale_silus(1)

    def g_col(i, a=0, b=P):
        return gains[a:b, i:i + 1]

    def h_gain(rnd, ft):
        return mix0_gain[:, ft:ft + 1] if rnd == 0 else g_col({1: G_FFN0, 2: G_MIX1, 3: G_FFN1}[rnd] + ft)

    K_MEAN_BANKS = (4, 5, 3, 7)
    SCORE_ORDER = (3, 2, 0, 1)

    def p_cols(i):
        c0 = P * (i * (i + 1) // 2)
        return slice(c0, c0 + P * (i + 1))

    def q_sq(h):
        return sq[:, h % 2, :] if h % 4 < 2 else sq_more[:, h % 2, :]

    def score(i):
        bank, c0 = ((1, 384), (2, 0), (1, 0), (0, 0))[i]
        return ps[:, bank, c0:c0 + P * (i + 1)]

    @block.scalar
    def _(act):
        x_quarter(act, 1)
        act.dma_start(mix0_gain[:, :], mix_norm[0].rearrange("(t p) -> p t", p=P),
                      allow_slow_non_contiguous=True).then_inc(mix0_loaded, 16)
        x_quarter(act, 3)

        nxt = [0]

        def hi(n, shift=0, count=None):
            s = n % W_SLOTS
            if n >= W_SLOTS:
                act.wait_ge(load_used, n - W_SLOTS + 1 + shift)
            if count is None:
                act.wait_ge(raw_landed[n % 2], landed(n))
            else:
                act.wait_ge(raw_landed[n % 2], count)
            if O_CKV <= n < O_CV:
                act.wait_ge(kr_columns, n - O_CKV + 1)
            if n in O_UQ:
                act.wait_ge(uq_columns, O_UQ.index(n) + 1)
            pairs = list(zip(ordered(n, w_hi[:, s, :], None), ordered(n, None, raw[:, n % 2, :])))
            for dst, src in pairs:
                ins = act.activation(dst, src, ACT.Copy)
            ins.then_inc(hi_done, 1)

        def through(p):
            while nxt[0] <= min(p + LEAD, N_LOADS - 1):
                hi(nxt[0])
                nxt[0] += 1

        def exp_table():
            act.activation(spare[:, :], eps_col[:, :], ACT.Exp)

        def rms_table():
            act.activation(spare[:, :], eps_col[:, :], ACT.Abs_reciprocal_sqrt)

        def h_high(rnd, ft):
            act.wait_ge(x_ready, 8 * rnd + ft + 1)
            act.activation(h_hi[:, ft, :], xT[:, ft, :], ACT.Copy, scale=h_gain(rnd, ft)).then_inc(h_hi_ready, 1)

        def h_square(rnd, ft):
            f = 8 * rnd + ft
            if ft >= 2:
                act.wait_ge(h_summed, f - 1)
            act.activation(sq[:, ft % 2, :], xT[:, ft, :], ACT.Square).then_inc(h_squared, 1)

        def fin(rnd, ft):
            h_high(rnd, ft)
            h_square(rnd, ft)

        def rms(m, src, n):
            act.wait_ge(sums_ready, m + 1)
            if m >= 2:
                act.wait_ge(rs_ready, m - 1)
            act.activation(y0[:, m % 2, :], src, ACT.Abs_reciprocal_sqrt, bias=eps_col[:, :], scale=1.0 / n
                           ).then_inc(rs_first, 1)
            if m >= 2 and used_before(m - 2):
                act.wait_ge(rs_used, used_before(m - 2))
            act.wait_ge(rs_first, m + 1)
            act.activation(rs[:, m % 2, :], y0[:, m % 2, :], ACT.Square, scale=float((0.5 / n) ** 0.5)
                           ).then_inc(rs_square, 1)

        act.wait_ge(columns_set, 1)
        rms_table()
        act.wait_ge(mix0_loaded, 16)
        h_high(0, 0)
        h_high(0, 1)
        through(-4)
        h_square(0, 0)
        h_square(0, 1)
        for ft in range(2, DT):
            fin(0, ft)
            if ft % 2:
                through(-4 + ft // 2)
        through(1)
        rms(M_MIX0, ps[:, 4, :], D)
        through(3)
        for j in range(4):
            act.wait_ge(e_q_scaled, j + 1)
            act.activation(yb[:, j, :], e_q[:, j, :], ACT.Square).then_inc(e_q_squared, 1)
        through(4)
        act.wait_ge(gains_turned, 1)
        for c, scale in ((slice(0, G_OQE), 1.0), (slice(G_OQE, G_OQO + 1), O_SCALE), (slice(G_OQO + 1, N_GAINS), 1.0)):
            act.activation(gains[:, c], ps[:, 7, c], ACT.Copy, scale=scale).then_inc(gains_ready, 1)
        through(5)
        act.wait_ge(e_k_scaled, 1)
        act.activation(sq[:, 0, :], e_k[:, :], ACT.Square).then_inc(e_k_squared, 1)
        rms(M_EQ, ps[:, 6, :], 1)
        rms(M_EQ + 1, ps[:, 7, :], 1)
        through(6)
        rms(M_EQ + 2, ps[:, 6, :], 1)
        rms(M_EQ + 3, ps[:, 7, :], 1)
        through(7)
        rms(M_EK, ps[:, 4, :], 1)
        act.wait_ge(e_v_turned, 1)
        act.activation(e_v[:, :, :], ps[:, 5, :].rearrange("p (t c) -> p t c", t=QT), ACT.Copy).then_inc(e_v_ready, 1)
        def e_exp(i):
            lo, o = (128 if i == 0 else 0), 8 * (i % 2)
            if i == 0:
                exp_table()
            act.wait_ge(a_neg_max, i + 1)
            act.wait_ge(a_sink_diff, i + 1)
            for h in range(HEADS):
                act.activation(e_sc[:, i % 2, h, lo:], e_sc[:, i % 2, h, lo:], ACT.Exp,
                               bias=tiny[:, o + 1, h:h + 1],
                               accum_out=tiny[:, o + 3, h:h + 1]).then_inc(a_exp_done, 1)
            act.activation(tiny[:, o + 4, :], tiny[:, o + 2, :], ACT.Exp).then_inc(a_sink_exp, 1)

        def e_out(i):
            act.wait_ge(a_values, i + 1)
            act.activation(yb[:, :, i * P:(i + 1) * P], ps[:, 4, :].rearrange("p (j q) -> p j q", j=4), ACT.Copy
                           ).then_inc(a_out, 1)
            act.wait_ge(a_out, i + 1)
            if i >= 2:
                act.wait_ge(yb_summed, i - 1)
            act.activation(sq[:, i % 2, :].rearrange("p (j q) -> p j q", j=4), yb[:, :, i * P:(i + 1) * P], ACT.Square
                           ).then_inc(yb_squared, 1)

        through(8)
        e_exp(0)
        through(10)
        act.wait_ge(a_probs_turned, 1)
        for kv in range(2):
            act.activation(e_pT[:, 2 * kv + 1, :], ps[:, 5 + 2 * kv, :], ACT.Copy).then_inc(a_pT_act, 1)
        e_exp(1)
        through(11)
        e_out(0)
        through(12)
        e_exp(2)
        through(13)
        e_out(1)
        for j in range(4):
            act.wait_ge(conv_h_ready, j + 1)
            act.activation(conv_y[:, j, :], conv_h[:, j, :], ACT.Copy, scale=g_col(G_CONV + 8 + j)).then_inc(conv_tap_a, 1)
        e_exp(3)
        rms_table()
        through(14)
        e_out(2)
        through(15)
        e_out(3)
        through(16)
        rms(M_EB, ps[:, 5, :], 512)
        for j0 in (0, 2):
            for j in (j0, j0 + 1):
                act.wait_ge(yb_normed, j + 1)
                act.activation(yb_hi[:, j, :], yb[:, j, :], ACT.Copy).then_inc(yb_hi_ready, 1)
            for j in (j0, j0 + 1):
                act.wait_ge(ya_ready, j + 1)
                if j >= 2:
                    act.wait_ge(ya_summed, j - 1)
                act.activation(sq[:, j % 2, :], conv_y[:, j, :], ACT.Square).then_inc(ya_squared, 1)
        through(17)
        through(18)
        rms(M_EA, ps[:, 0, :], 512)
        for j in range(4):
            act.wait_ge(ya_normed, j + 1)
            act.activation(ya_hi[:, j, :], conv_y[:, j, :], ACT.Copy).then_inc(ya_hi_ready, 1)

        def residual(rnd, out0):
            through(out0 + 3)
            for ft in range(4):
                fin(rnd, ft)
            through(out0 + 7)
            for ft in range(4, 8):
                fin(rnd, ft)


        def ffn(layer, bank0):
            n0, n1 = FFN_IN[layer], FFN_OUT[layer]
            c = 22 * layer
            through(n0 + 1)
            rms(M_FFN0 if layer == 0 else M_FFN1, ps[:, (1 - bank0) * 4, :], D)
            through(n0 + 3)

            def group(t0, dst, shift):
                for t in range(2):
                    act.wait_ge(gate_scaled, c + t0 + t + 1 + shift)
                    b = (t0 + t) % 4
                    act.activation(ffn_t[:, b, :], ffn_t[:, b, :], ACT.Silu).then_inc(silu_done, 1)
                for t in range(2):
                    act.wait_ge(hidden_ready, 1 + c + t0 + t + 1 + shift)
                    act.activation(dst[:, t, :], ffn_t[:, (t0 + t) % 4, :], ACT.Copy).then_inc(hidden_hi, 1)

            group(0, act_hi[:, 0:2, :], 0)
            with act.Fori(0, NG_FF // 2) as i:
                for g in (1, 2):
                    for j in range(4):
                        n = n0 + 4 * g + 4 + j
                        hi(n, 8 * i, landed(n) + 64 * i)
                    group(2 * g, act_hi[:, bass.ds(4 * i + 2 * g, 2), :], 4 * i)
            nxt[0] = n1 + 4
            n = nxt[0]
            through(n1 + 2)
            with act.Fori(0, 2) as i:
                for j in range(4):
                    hi(n + 3 + j, 4 * i, landed(n + 3 + j) + 32 * i)
            nxt[0] = n + 11

        residual(1, E_OUT)
        ffn(0, 1)
        for ft in range(4):
            fin(2, ft)
        through(FFN_OUT[0] + 21)
        for ft in range(4, 8):
            fin(2, ft)

        through(O_CQ + 1)
        rms(M_MIX1, ps[:, 4, :], D)
        act.wait_ge(tok_sums, 1)
        act.activation(tiny[:, 0, 0:4], ps[:, 5, 0:4], ACT.Abs_reciprocal_sqrt, bias=eps_col[:, :], scale=1.0 / D
                       ).then_inc(tok_first, 1)
        act.wait_ge(tok_first, 1)
        act.activation(tiny[:, 5, 0:4], tiny[:, 0, 0:4], ACT.Square, scale=float((0.5 / D) ** 0.5)
                       ).then_inc(tok_square, 1)
        through(O_CQ + 3)
        for j in range(3):
            act.wait_ge(cq_scaled, j + 1)
            if j >= 2:
                act.wait_ge(cq_summed, j - 1)
            act.activation(sq[:, j % 2, :], cq[:, j, :], ACT.Square).then_inc(cq_squared, 1)
        through(O_CQ + 4)
        rms(M_CQ, ps[:, 3, :], 384)
        for j in range(3):
            act.wait_ge(cq_normed, j + 1)
            act.activation(cq_hi[:, j, :], cq[:, j, :], ACT.Copy).then_inc(cq_hi_ready, 1)
        through(O_CKV + 3)
        for j in range(2):
            act.wait_ge(ckv_scaled, j + 1)
            act.activation(sq[:, j, :], ckv[:, j, :], ACT.Square).then_inc(ckv_squared, 1)
        act.wait_ge(ckv_scaled, 3)
        act.wait_ge(ckv_summed, 2)
        act.activation(sq[:, 0, :], kr[:, 0, :], ACT.Square).then_inc(ckv_squared, 1)
        through(O_CV)
        rms(M_CKV, ps[:, 4, :], 256)
        for j in range(2):
            act.wait_ge(ckv_normed, j + 1)
            act.activation(ckv_hi[:, j, :], ckv[:, j, :], ACT.Copy).then_inc(ckv_hi_ready, 1)
        rms(M_KR, ps[:, 5, :], P)
        through(O_CV + 2)
        act.wait_ge(ckv_lo_ready, 2)
        for b in range(2):
            act.wait_ge(spatial_turned, b + 1)
            act.activation(w_spT[:, 4 * b:4 * b + 4, :], ps[:, 6 + b, :].rearrange("p (g i) -> p g i", g=4), ACT.Copy
                           ).then_inc(spatial_ready, 1)
        through(O_CV + 3)
        act.wait_ge(tok_scale, 1)
        act.wait_ge(load_used, O_CV + 4)
        for t in range(QT):
            act.activation(v_c[:, t, :], ps[:, t, :], ACT.Gelu_apprx_tanh, scale=tiny[:, 6, t:t + 1]).then_inc(cv_ready, 1)

        def q_squares(j, b0):
            act.wait_ge(load_used, O_UQ[j] + 1)
            for i in range(2):
                h = 2 * j + i
                if h >= 4:
                    act.wait_ge(sums_ready, M_OQ + h - 3)
                elif h >= 2:
                    act.wait_ge(spatial_turned, 2)
                act.activation(q_sq(h), ps[:, b0 + i, :], ACT.Square).then_inc(oq_squared, 1)

        q_squares(0, 4)
        q_squares(1, 6)
        through(105)
        rms(M_OQ, ps[:, 4, :], 1)
        rms(M_OQ + 1, ps[:, 5, :], 1)
        through(106)
        rms(M_OQ + 2, ps[:, 6, :], 1)
        rms(M_OQ + 3, ps[:, 7, :], 1)
        through(107)
        act.wait_ge(kr_rotated, 1)
        for t in range(QT):
            act.wait_ge(cv_ready, t + 1)
            if t:
                act.wait_ge(cv_squared, t)
            act.activation(kr[:, 0, :], v_c[:, t, :], ACT.Square, accum_out=tiny[:, 7, t:t + 1]).then_inc(cv_squared, 1)
        act.wait_ge(cv_squared, QT)
        act.activation(tiny[:, 8, 0:4], tiny[:, 7, 0:4], ACT.Abs_reciprocal_sqrt, bias=eps_col[:, :], scale=1.0 / 512
                       ).then_inc(cv_first, 1)
        act.wait_ge(cv_first, 1)
        act.activation(tiny[:, 13, 0:4], tiny[:, 8, 0:4], ACT.Square, scale=float((0.5 / 512) ** 0.5)
                       ).then_inc(cv_square, 1)
        q_squares(2, 4)
        q_squares(3, 6)
        through(109)
        rms(M_OQ + 4, ps[:, 4, :], 1)
        rms(M_OQ + 5, ps[:, 5, :], 1)
        through(110)
        rms(M_OQ + 6, ps[:, 6, :], 1)
        rms(M_OQ + 7, ps[:, 7, :], 1)
        for j in range(4):
            act.wait_ge(u_scaled, j + 1)
            act.activation(u_c[:, j, :], u_c[:, j, :], ACT.Gelu_apprx_tanh).then_inc(u_ready, 1)
        through(111)

        def kv_tiles(half):
            act.wait_ge(load_used, O_UKV + half + 1)
            for j in range(2):
                act.wait_ge(sums_ready, M_OK + 2 * half + j - 1)
                act.activation(sq[:, j, :], ps[:, 4 + j, :], ACT.Square).then_inc(ok_squared, 1)
            act.activation(o_v[:, 0:2, 256 * half:256 * half + 256],
                           ps[:, 6, :].rearrange("p (t c) -> p t c", t=2), ACT.Copy).then_inc(ov_act, 1)

        kv_tiles(0)
        through(112)
        rms(M_OK, ps[:, 4, :], 1)
        rms(M_OK + 1, ps[:, 5, :], 1)
        kv_tiles(1)
        through(113)

        def yc_square(j):
            act.wait_ge(yc_ready, j + 1)
            if j < 2:
                act.wait_ge(sums_ready, M_OK + 3 + j)
            else:
                act.wait_ge(yc_summed, j - 1)
            act.activation(sq[:, j % 2, :], yc[:, j, :], ACT.Square).then_inc(yc_squared, 1)

        def o_exp(h):
            o = 8 * (h % 2)
            if h == 1:
                exp_table()
                act.wait_ge(rs_used, used_before(M_OK + 1))
            if h >= 2:
                act.wait_ge(d_probs_turned, h - 1)
            act.wait_ge(d_neg_max, QT * h + 1)
            for n, i in enumerate(SCORE_ORDER):
                if n:
                    act.wait_ge(d_neg_max, QT * h + (1, 3, 3, 4)[n])
                act.activation(o_p[:, h % 2, p_cols(i)], score(i), ACT.Exp,
                               bias=tiny[:, o + 1, i:i + 1],
                               accum_out=tiny[:, o + 2, i:i + 1]).then_inc(d_exp_done, 1)

        def o_out(h):
            a, j = 64 * (h % 2), h // 2
            act.wait_ge(d_values, h + 1)
            act.activation(yd[a:a + 64, j, :], ps[a:a + 64, 7, :], ACT.Copy).then_inc(d_out, 1)
            if h % 2:
                act.wait_ge(d_out, h + 1)
                if j >= 2:
                    act.wait_ge(yd_summed, j - 1)
                act.activation(sq[:, j % 2, :], yd[:, j, :], ACT.Square).then_inc(yd_squared, 1)

        o_exp(0)
        rms(M_OK + 2, ps[:, 3, :], 1)
        rms(M_OK + 3, ps[:, 7, :], 1)
        for h in range(HEADS):
            if 1 <= h < 6:
                o_exp(h + 1)
            if h >= 1:
                o_out(h - 1)
            act.wait_ge(d_probs_turned, h + 1)
            act.activation(o_pT[:, 0, :], ps[:, 4, :], ACT.Copy).then_inc(d_pT_act, 1)
            act.activation(o_pT[:, 2, 0:256], ps[:, 6, 0:256], ACT.Copy).then_inc(d_pT_act, 1)
            if h == 0 or h == 6:
                o_exp(h + 1)
            if h == 6:
                rms_table()
            if h == 0:
                for j in range(4):
                    yc_square(j)
            if h == 2:
                rms(M_OC, ps[:, 3, :], 512)
            if 3 <= h < 7:
                act.wait_ge(yc_normed, h - 2)
                act.activation(yc_hi[:, h - 3, :], yc[:, h - 3, :], ACT.Copy).then_inc(yc_hi_ready, 1)
        o_out(7)
        through(O_OUT)
        rms(M_OD, ps[:, 4, :], 512)
        for j in range(4):
            act.wait_ge(yd_normed, j + 1)
            act.activation(yd_hi[:, j, :], yd[:, j, :], ACT.Copy).then_inc(yd_hi_ready, 1)
        residual(3, O_OUT)
        ffn(1, 0)
        for half in range(2):
            if half:
                through(N_LOADS - 1)
            for t in (0, 2):
                act.wait_ge(out_turned, 4 * half + t + 1)
                act.activation(out_tok[:, t, 512 * half:512 * half + 512], ps[:, 4 + t, :], ACT.Copy).then_inc(out_act, 1)

    @block.vector
    def _(dve):
        TT, STT, TS, TC = dve.tensor_tensor, dve.scalar_tensor_tensor, dve.tensor_scalar, dve.tensor_copy
        nxt = [0]

        def lo(n, shift=0):
            s = n % W_SLOTS
            dve.wait_ge(hi_done, n + 1 + shift)
            parts = zip(ordered(n, w_lo[:, s, :], None), ordered(n, None, raw[:, n % 2, :]),
                        ordered(n, w_hi[:, s, :].bitcast(F32), None))
            for dst, src, high in parts:
                ins = TT(dst, src, high, ALU.subtract)
            ins.then_inc(lo_done, 1)

        def through(p):
            while nxt[0] <= min(p + LEAD, N_LOADS - 1):
                lo(nxt[0])
                nxt[0] += 1

        def low(dst, src, high, done):
            TT(dst, src, high.bitcast(F32), ALU.subtract).then_inc(done, 1)

        def fin(rnd, ft):
            h_low(rnd, ft)
            h_sum(rnd, ft)

        def h_low(rnd, ft):
            f = 8 * rnd + ft
            dve.wait_ge(h_hi_ready, f + 1)
            STT(out=h_lo[:, ft, :], in0=xT[:, ft, :], scalar=h_gain(rnd, ft), in1=h_hi[:, ft, :].bitcast(F32),
                op0=ALU.mult, op1=ALU.subtract).then_inc(h_lo_ready, 1)

        def h_sum(rnd, ft):
            f = 8 * rnd + ft
            dve.wait_ge(h_squared, f + 1)
            if ft == 0:
                if rnd:
                    dve.wait_ge(sums_ready, (M_MIX0, M_EA, M_FFN0, M_OD)[rnd] + 1)
                TC(acc[:, :], sq[:, 0, :]).then_inc(h_summed, 1)
            else:
                dve.wait_ge(h_summed, f)
                TT(acc[:, :], acc[:, :], sq[:, ft % 2, :], ALU.add).then_inc(h_summed, 1)

        def sum_squares(squared, summed, count, read_by):
            for j in range(count):
                dve.wait_ge(squared, j + 1)
                if j == 0:
                    dve.wait_ge(sums_ready, read_by + 1)
                    TC(acc[:, :], sq[:, 0, :]).then_inc(summed, 1)
                else:
                    dve.wait_ge(summed, j)
                    TT(acc[:, :], acc[:, :], sq[:, j % 2, :], ALU.add).then_inc(summed, 1)

        def rms(m, src, n):
            b = m % 2
            dve.wait_ge(rs_square, m + 1)
            STT(out=rs[:, b, :], in0=src, scalar=n * EPS, in1=rs[:, b, :], op0=ALU.add, op1=ALU.mult
                ).then_inc(rs_step, 1)
            dve.wait_ge(rs_step, m + 1)
            dst = row_scale[:, :] if m in TO_ROW_SCALE else rs[:, b, :]
            STT(out=dst, in0=rs[:, b, :], scalar=1.5, in1=y0[:, b, :], op0=ALU.subtract, op1=ALU.mult, reverse0=True
                ).then_inc(rs_ready, 1)
            dve.wait_ge(rs_ready, m + 1)
            return rs[:, b, :]

        def normed(tiles, gain0, r, count, done, high, low_, high_done, low_done, between=None):
            for j0 in range(0, count, 2):
                two = range(j0, min(j0 + 2, count))
                for j in two:
                    STT(out=tiles[:, j, :], in0=tiles[:, j, :], scalar=g_col(gain0 + j), in1=r,
                        op0=ALU.mult, op1=ALU.mult).then_inc(done, 1)
                for j in two:
                    dve.wait_ge(high_done, j + 1)
                    low(low_[:, j, :], tiles[:, j, :], high[:, j, :], low_done)
                if j0 == 0 and between:
                    between()
            dve.sem_inc(rs_used, 1)

        dve.sem_inc(hidden_ready, 1)
        dve.wait_ge(small_loaded, 16)
        def x_copy(ft):
            dve.wait_ge(x_turned, ft + 1)
            TC(xT[:, ft, :], ps[:, ft, :]).then_inc(x_ready, 1)

        for ft in range(4):
            x_copy(ft)
        h_low(0, 0)
        h_low(0, 1)
        through(-4)
        h_sum(0, 0)
        h_sum(0, 1)
        x_copy(4)
        for ft in range(2, DT):
            fin(0, ft)
            if ft % 2:
                through(-4 + ft // 2)
            if ft < 5:
                x_copy(ft + 3)
        through(1)
        rms(M_MIX0, ps[:, 4, :], D)
        through(3)
        dve.wait_ge(load_used, E_Q + 4)
        for j in range(4):
            TT(e_q[:, j, :], ps[:, j, :], row_scale[:, :], ALU.mult).then_inc(e_q_scaled, 1)
        through(5)
        dve.wait_ge(load_used, E_KV + 2)
        TT(e_k[:, :], ps[:, 4, :], row_scale[:, :], ALU.mult).then_inc(e_k_scaled, 1)
        TT(e_vT[:, :], ps[:, 5, :], row_scale[:, :], ALU.mult).then_inc(e_v_scaled, 1)

        def e_norm(m, bank, tile, gain):
            r = rms(m, ps[:, bank, :], 1)
            STT(out=tile, in0=tile, scalar=g_col(gain), in1=r, op0=ALU.mult, op1=ALU.mult).then_inc(rs_used, 1)

        dve.wait_ge(gains_ready, 3)
        e_norm(M_EQ, 6, e_q[:, 0, :], G_EQ)
        e_norm(M_EQ + 1, 7, e_q[:, 1, :], G_EQ)
        through(6)
        e_norm(M_EQ + 2, 6, e_q[:, 2, :], G_EQ)
        e_norm(M_EQ + 3, 7, e_q[:, 3, :], G_EQ)
        through(7)
        e_norm(M_EK, 4, e_k[:, :], G_EK)
        dve.wait_ge(alibi_loaded, 16)
        dve.wait_ge(sinks_loaded, 16)

        def e_max(i):
            lo_, o, b0 = (128 if i == 0 else 0), 8 * (i % 2), 4
            dve.wait_ge(a_scores, i + 1)
            if i >= 2:
                dve.wait_ge(a_probs_turned, i - 1)
            sc = e_sc[:, i % 2]
            for b in range(4):
                scale_and_bias(sc[:, 2 * b:2 * b + 2, lo_:], ps[:, b0 + b, :].rearrange("p (h k) -> p h k", h=2)[:, :, lo_:],
                     alibi[:, 2 * b:2 * b + 2, lo_:])
            dve.wait_ge(a_biased, 4 * (i + 1))
            dve.tensor_reduce(tiny[:, o, :], sc[:, :, lo_:], AX, ALU.max).then_inc(a_row_max, 1)
            dve.wait_ge(a_row_max, i + 1)
            TT(tiny[:, o, :], tiny[:, o, :], sinks[:, :], ALU.max).then_inc(a_max, 1)
            dve.wait_ge(a_max, i + 1)
            TS(tiny[:, o + 1, :], tiny[:, o, :], -1.0, None, ALU.mult).then_inc(a_neg_max, 1)
            TT(tiny[:, o + 2, :], sinks[:, :], tiny[:, o, :], ALU.subtract).then_inc(a_sink_diff, 1)

        def scale_and_bias(dst, scores, penalty):
            STT(out=dst, in0=scores, scalar=E_SCALE, in1=penalty, op0=ALU.mult, op1=ALU.add).then_inc(a_biased, 1)

        def e_prob(i):
            lo_, o = (128 if i == 0 else 0), 8 * (i % 2)
            dve.wait_ge(a_sink_exp, i + 1)
            TT(tiny[:, o + 5, :], tiny[:, o + 3, :], tiny[:, o + 4, :], ALU.add).then_inc(a_denominator, 1)
            dve.wait_ge(a_denominator, i + 1)
            dve.reciprocal(tiny[:, o + 6, :], tiny[:, o + 5, :]).then_inc(a_inverse, 1)
            dve.wait_ge(a_inverse, i + 1)
            for h in range(HEADS):
                TS(e_sc[:, i % 2, h, lo_:], e_sc[:, i % 2, h, lo_:], tiny[:, o + 6, h:h + 1], None, ALU.mult
                   ).then_inc(a_probs, 1)

        def e_pt(i):
            dve.wait_ge(a_probs_turned, i + 1)
            dve.wait_ge(a_values, i)
            for b in range(4):
                TC(e_pT[:, b, :], ps[:, 4 + b, :]).then_inc(a_pT_dve, 1)

        def e_sum(i):
            dve.wait_ge(yb_squared, i + 1)
            dve.tensor_reduce(acc[:, i * P:(i + 1) * P], sq[:, i % 2, :].rearrange("p (j q) -> p q j", j=4), AX, ALU.add
                              ).then_inc(yb_summed, 1)

        through(8)
        e_max(0)
        dve.wait_ge(load_used, E_AIN + 4)
        for j in range(4):
            TT(conv_h[:, j, :], ps[:, j, :], row_scale[:, :], ALU.mult).then_inc(conv_in_scaled, 1)
        e_prob(0)
        through(9)
        e_max(1)
        through(10)
        e_prob(1)
        through(11)
        dve.wait_ge(sums_ready, M_MIX0 + 1)
        e_sum(0)
        e_max(2)
        e_pt(1)
        through(12)
        e_prob(2)
        dve.wait_ge(load_used, E_AC + 4)
        for j in range(4):
            dve.wait_ge(conv_in_ready, j + 1)
            TT(conv_h[:, j, :], ps[:, j, :], conv_h[:, j, :], ALU.mult).then_inc(conv_h_ready, 1)
        through(13)
        e_sum(1)
        e_max(3)
        for j in range(4):
            dve.wait_ge(conv_tap_a, j + 1)
            STT(out=conv_y[:, j, 1:], in0=conv_h[:, j, 0:S - 1], scalar=g_col(G_CONV + 4 + j), in1=conv_y[:, j, 1:],
                op0=ALU.mult, op1=ALU.add).then_inc(conv_tap_b, 1)
        e_pt(2)
        e_prob(3)
        through(14)
        for j in range(4):
            dve.wait_ge(conv_tap_b, j + 1)
            STT(out=conv_y[:, j, 2:], in0=conv_h[:, j, 0:S - 2], scalar=g_col(G_CONV + j), in1=conv_y[:, j, 2:],
                op0=ALU.mult, op1=ALU.add).then_inc(conv_tap_c, 1)
        e_pt(3)
        e_sum(2)
        through(15)
        e_sum(3)
        through(16)
        r = rms(M_EB, ps[:, 5, :], 512)

        def ya_tiles():
            dve.wait_ge(load_used, E_AB + 4)
            for j in range(4):
                dve.wait_ge(conv_y_scaled, j + 1)
                TT(conv_y[:, j, :], ps[:, j, :], conv_y[:, j, :], ALU.mult).then_inc(ya_ready, 1)

        normed(yb, G_EB, r, 4, yb_normed, yb_hi, yb_lo, yb_hi_ready, yb_lo_ready, ya_tiles)
        sum_squares(ya_squared, ya_summed, 4, M_EB)
        through(17)
        through(18)
        r = rms(M_EA, ps[:, 0, :], 512)
        normed(conv_y, G_EA, r, 4, ya_normed, ya_hi, ya_lo, ya_hi_ready, ya_lo_ready)

        def add_x(rnd, last_load, ft0, bank0):
            dve.wait_ge(load_used, last_load + 1)
            for j in range(4):
                TT(xT[:, ft0 + j, :], ps[:, bank0 + j, :], xT[:, ft0 + j, :], ALU.add).then_inc(x_ready, 1)
                if 0 < j and rnd < 4:
                    fin(rnd, ft0 + j - 1)
            if rnd < 4:
                fin(rnd, ft0 + 3)

        def residual(rnd, out0, bank0):
            through(out0 + 3)
            add_x(rnd, out0 + 3, 0, bank0)
            through(out0 + 7)
            add_x(rnd, out0 + 7, 4, 4 - bank0)

        def ffn(layer, bank0):
            n0, n1 = FFN_IN[layer], FFN_OUT[layer]
            c = 22 * layer
            through(n0 + 1)
            rms(M_FFN0 if layer == 0 else M_FFN1, ps[:, (1 - bank0) * 4, :], D)
            through(n0 + 3)

            def group(t0, b0, load, dst_hi, dst_lo, shift, load_shift):
                dve.wait_ge(load_used, load + 4 + load_shift)
                for t in range(2):
                    TT(ffn_t[:, (t0 + t) % 4, :], ps[:, b0 + t, :], row_scale[:, :], ALU.mult).then_inc(gate_scaled, 1)
                for t in range(2):
                    b = (t0 + t) % 4
                    dve.wait_ge(silu_scaled, c + t0 + t + 1 + shift)
                    TT(ffn_t[:, b, :], ps[:, b0 + 2 + t, :], ffn_t[:, b, :], ALU.mult).then_inc(hidden_ready, 1)
                for t in range(2):
                    dve.wait_ge(hidden_hi, c + t0 + t + 1 + shift)
                    TT(dst_lo[:, t, :], ffn_t[:, (t0 + t) % 4, :], dst_hi[:, t, :].bitcast(F32), ALU.subtract
                       ).then_inc(hidden_lo, 1)

            group(0, 4 * bank0, n0, act_hi[:, 0:2, :], act_lo[:, 0:2, :], 0, 0)
            with dve.Fori(0, NG_FF // 2) as i:
                for g in (1, 2):
                    for j in range(4):
                        lo(n0 + 4 * g + 4 + j, 8 * i)
                    t = bass.ds(4 * i + 2 * g, 2)
                    group(2 * g, 4 * ((bank0 + g) % 2), n0 + 4 * g, act_hi[:, t, :], act_lo[:, t, :], 4 * i, 8 * i)
            nxt[0] = n1 + 4
            n = nxt[0]
            through(n1 + 2)
            with dve.Fori(0, 2) as i:
                for j in range(4):
                    lo(n + 3 + j, 4 * i)
            nxt[0] = n + 11

        residual(1, E_OUT, 4)
        ffn(0, 1)
        add_x(2, FFN_OUT[0] + 10, 0, 0)
        through(FFN_OUT[0] + 21)
        add_x(2, FFN_OUT[0] + 21, 4, 4)

        through(O_CQ + 1)
        rms(M_MIX1, ps[:, 4, :], D)
        dve.wait_ge(tok_square, 1)
        STT(out=tiny[:, 5, 0:4], in0=ps[:, 5, 0:4], scalar=D * EPS, in1=tiny[:, 5, 0:4], op0=ALU.add, op1=ALU.mult
            ).then_inc(tok_step, 1)
        dve.wait_ge(tok_step, 1)
        STT(out=tiny[:, 6, 0:4], in0=tiny[:, 5, 0:4], scalar=1.5, in1=tiny[:, 0, 0:4], op0=ALU.subtract, op1=ALU.mult,
            reverse0=True).then_inc(tok_scale, 1)
        through(O_CQ + 3)
        dve.wait_ge(load_used, O_CQ + 4)
        for j in range(3):
            TT(cq[:, j, :], ps[:, j, :], row_scale[:, :], ALU.mult).then_inc(cq_scaled, 1)
        sum_squares(cq_squared, cq_summed, 3, M_MIX1)
        through(O_CQ + 4)
        r = rms(M_CQ, ps[:, 3, :], 384)
        normed(cq, G_CQ, r, 3, cq_normed, cq_hi, cq_lo, cq_hi_ready, cq_lo_ready)
        through(O_CKV + 3)
        dve.wait_ge(load_used, O_CKV + 4)
        for j in range(2):
            TT(ckv[:, j, :], ps[:, 4 + j, :], row_scale[:, :], ALU.mult).then_inc(ckv_scaled, 1)
        TT(kr[:, 0, :], ps[:, 6, :], row_scale[:, :], ALU.mult).then_inc(ckv_scaled, 1)
        sum_squares(ckv_squared, ckv_summed, 2, M_CQ)
        through(O_CV)
        r = rms(M_CKV, ps[:, 4, :], 256)
        normed(ckv, G_CKV, r, 2, ckv_normed, ckv_hi, ckv_lo, ckv_hi_ready, ckv_lo_ready)
        r = rms(M_KR, ps[:, 5, :], P)
        dve.wait_ge(tables_loaded, 16)
        STT(out=kr[:, 0, :], in0=kr[:, 0, :], scalar=g_col(G_KR), in1=r, op0=ALU.mult, op1=ALU.mult).then_inc(kr_normed, 1)
        dve.wait_ge(kr_normed, 1)
        dve.sem_inc(rs_used, 1)
        TT(kr[:, 0, :], kr[:, 0, :], tables[:, TAB_KEY:TAB_KEY + S], ALU.mult).then_inc(kr_terms, 1)
        through(O_CV + 2)
        dve.wait_ge(kr_added, 1)
        TC(kr[:, 1, :], ps[:, 5, :]).then_inc(kr_rotated, 1)
        through(O_CV + 3)
        def q_tiles(j, b0):
            for i in range(2):
                h = 2 * j + i
                dve.wait_ge(oq_squared, h + 1)
                tab = TAB_ODD if h % 2 else TAB_EVEN
                STT(out=o_q[:, h, :], in0=ps[:, b0 + i, :], scalar=g_col(G_OQO if h % 2 else G_OQE),
                    in1=tables[:, tab:tab + S], op0=ALU.mult, op1=ALU.mult).then_inc(oq_turned, 1)

        def q_norm(j, b0):
            rms(M_OQ + 2 * j, ps[:, b0, :], 1)
            rms(M_OQ + 2 * j + 1, ps[:, b0 + 1, :], 1)

        q_tiles(0, 4)
        q_tiles(1, 6)
        through(105)
        q_norm(0, 4)
        through(106)
        q_norm(1, 6)
        through(107)
        q_tiles(2, 4)
        q_tiles(3, 6)
        dve.wait_ge(cv_square, 1)
        TS(tiny[:, 7, 0:4], tiny[:, 7, 0:4], 512 * EPS, None, ALU.add).then_inc(cv_step, 1)
        dve.wait_ge(cv_step, 1)
        TT(tiny[:, 13, 0:4], tiny[:, 7, 0:4], tiny[:, 13, 0:4], ALU.mult).then_inc(cv_step, 1)
        dve.wait_ge(cv_step, 2)
        STT(out=tiny[:, 15, 0:4], in0=tiny[:, 13, 0:4], scalar=1.5, in1=tiny[:, 8, 0:4], op0=ALU.subtract, op1=ALU.mult,
            reverse0=True).then_inc(cv_scale, 1)
        dve.wait_ge(cv_scale, 1)
        for t in range(QT):
            TS(v_c[:, t, :], v_c[:, t, :], tiny[:, 15, t:t + 1], None, ALU.mult).then_inc(cv_normed, 1)
        through(109)
        q_norm(2, 4)
        through(110)
        q_norm(3, 6)
        dve.wait_ge(load_used, O_CU[3] + 1)
        for j in range(4):
            TT(u_c[:, j, :], ps[:, j, :], row_scale[:, :], ALU.mult).then_inc(u_scaled, 1)
        through(111)

        def kv_tiles(half):
            dve.wait_ge(load_used, O_UKV + half + 1)
            TC(o_v[:, 2:4, 256 * half:256 * half + 256], ps[:, 7, :].rearrange("p (t c) -> p t c", t=2)
               ).then_inc(ov_dve, 1)
            for j in range(2):
                dve.wait_ge(ok_squared, 2 * half + j + 1)
                TS(k_pairs[half][:, j, :], ps[:, 4 + j, :], g_col(G_OK), None, ALU.mult).then_inc(ok_gained, 1)

        def k_norm(half):
            for j in range(2):
                p = 2 * half + j
                r = rms(M_OK + p, ps[:, K_MEAN_BANKS[p], :], 1)
                dve.wait_ge(ok_gained, p + 1)
                TT(o_k[0:64, 2 * p, :], k_pairs[half][0:64, j, :], r[0:64, :], ALU.mult).then_inc(ok_normed, 1)

        kv_tiles(0)
        dve.wait_ge(gate_bias_loaded, 32)
        dve.wait_ge(gates_mixed, 1)
        dve.wait_ge(kr_copied, HEADS)
        for j in range(4):
            STT(out=yc[:, j, :].rearrange("p (n i) -> p n i", n=QT), in0=ps[:, j, :].rearrange("p (n i) -> p n i", n=QT),
                scalar=g_col(G_V + j), in1=gate_bias[:, j:j + 1, :].broadcast_to([P, QT, P]),
                op0=ALU.mult, op1=ALU.add).then_inc(gates_ready, 1)
        k_norm(0)
        through(112)
        kv_tiles(1)
        def o_max(h):
            o = 8 * (h % 2)
            for n, i in enumerate(SCORE_ORDER):
                dve.wait_ge(d_scores, QT * h + (1, 3, 3, 4)[n])
                dve.tensor_reduce(tiny[:, o + 1, i:i + 1], score(i), AX, ALU.max, negate=True).then_inc(d_neg_max, 1)

        def o_prob(h):
            o = 8 * (h % 2)
            dve.wait_ge(d_exp_done, QT * (h + 1))
            dve.reciprocal(tiny[:, o + 3, 0:4], tiny[:, o + 2, 0:4]).then_inc(d_inverse, 1)
            dve.wait_ge(d_inverse, h + 1)
            for i in range(QT):
                p = o_p[:, h % 2, p_cols(i)]
                TS(p, p, tiny[:, o + 3, i:i + 1], None, ALU.mult).then_inc(d_probs, 1)

        def yd_sum(j):
            dve.wait_ge(yd_squared, j + 1)
            if j:
                dve.wait_ge(yd_summed, j)
                TT(acc[:, :], acc[:, :], sq[:, j % 2, :], ALU.add).then_inc(yd_summed, 1)
            else:
                dve.wait_ge(sums_ready, M_OC + 1)
                TC(acc[:, :], sq[:, 0, :]).then_inc(yd_summed, 1)

        o_max(0)
        dve.wait_ge(gates_ready, 4)
        for j in range(4):
            dve.wait_ge(u_ready, j + 1)
            TT(yc[:, j, :], yc[:, j, :], u_c[:, j, :], ALU.mult).then_inc(yc_ready, 1)
        o_prob(0)
        o_max(1)
        k_norm(1)
        through(113)
        for h in range(HEADS):
            if h:
                o_prob(h)
            if 1 <= h < HEADS - 1:
                o_max(h + 1)
            dve.wait_ge(d_probs_turned, h + 1)
            if h:
                dve.wait_ge(d_values, h)
            TC(o_pT[:, 1, :], ps[:, 5, :]).then_inc(d_pT_dve, 1)
            if h == 0:
                sum_squares(yc_squared, yc_summed, 4, M_CKV)
            if h == 3:
                dve.wait_ge(rs_used, used_before(M_OK + 3))
                r_c = rms(M_OC, ps[:, 3, :], 512)
            if 3 <= h < 7:
                STT(out=yc[:, h - 3, :], in0=yc[:, h - 3, :], scalar=g_col(G_OOUT + h - 3), in1=r_c,
                    op0=ALU.mult, op1=ALU.mult).then_inc(yc_normed, 1)
            if 4 <= h:
                dve.wait_ge(yc_hi_ready, h - 3)
                low(yc_lo[:, h - 4, :], yc[:, h - 4, :], yc_hi[:, h - 4, :], yc_lo_ready)
            if h >= 3 and h % 2:
                yd_sum(h // 2 - 1)
            if h == 7:
                dve.wait_ge(yc_normed, 4)
                dve.sem_inc(rs_used, 1)
        yd_sum(3)
        through(O_OUT)
        r = rms(M_OD, ps[:, 4, :], 512)
        normed(yd, G_OOUT + 4, r, 4, yd_normed, yd_hi, yd_lo, yd_hi_ready, yd_lo_ready)
        residual(3, O_OUT, 0)
        ffn(1, 0)
        for half in range(2):
            b0 = 4 if half == 0 else 0
            if half:
                through(N_LOADS - 1)
            add_x(4, FFN_OUT[1] + 10 + 11 * half, 4 * half, b0)
            for t in (1, 3):
                dve.wait_ge(out_turned, 4 * half + t + 1)
                TC(out_tok[:, t, 512 * half:512 * half + 512], ps[:, 4 + t, :]).then_inc(out_dve, 1)

    @block.tensor
    def _(pe):
        MM = pe.matmul

        def product(dst, st_hi, st_lo, mv_hi, mv_lo, start, stop):
            MM(dst, st_hi, mv_hi, start=start, stop=False)
            MM(dst, st_hi, mv_lo, start=False, stop=False)
            return MM(dst, st_lo, mv_hi, start=False, stop=stop)

        def ready(n, shift=0):
            pe.wait_ge(lo_done, n + 1 + shift)

        def load(n, tiles, ks, moving, banks, first, last, shift=0, extra=None):
            ready(n, shift)
            hi_, lo_ = w_hi[:, n % W_SLOTS, :], w_lo[:, n % W_SLOTS, :]
            for kk, k in enumerate(ks):
                if kk and extra:
                    extra()
                mh, ml = moving(k)
                th, tl = tiles(hi_, kk), tiles(lo_, kk)
                for t, b in enumerate(banks):
                    ins = product(ps[0:P, b, :], th[t], tl[t], mh, ml,
                                  first and kk == 0, last and kk == len(ks) - 1)
            ins.then_inc(load_used, 1)

        def plain(cols, count):
            return lambda w, kk: [w[:, cols * kk + P * t:cols * kk + P * t + P] for t in range(count)]

        H = lambda k: (h_hi[:, k, :], h_lo[:, k, :])

        def mean(m, bank, weights, src):
            MM(ps[:, bank, :], weights, src, start=True, stop=True).then_inc(sums_ready, 1)

        pe.wait_ge(small_loaded, 16)
        for ft in range(DT):
            if ft % 2 == 0:
                pe.wait_ge(x_loaded[ft // 2], 16)
            for t in range(QT):
                ins = pe.transpose(ps[:, ft, t * P:(t + 1) * P], x_tok[:, t, ft * P:(ft + 1) * P], ident)
            ins.then_inc(x_turned, 1)

        def e_load(n, j, count, tiles, b0, per=2, extra=None):
            if n < E_Q + 4:
                pe.wait_ge(h_lo_ready, per * (j + 1))
            load(n, tiles, range(per * j, per * j + per), H, range(b0, b0 + count), j == 0, j == DT // per - 1, extra=extra)

        pe.wait_ge(x_ready, 4)
        for j in range(4):
            e_load(E_Q + j, j, 4, plain(512, 4), 0)
            if j == 2:
                pe.wait_ge(h_summed, 8)
                pe.wait_ge(x_ready, 8)
                mean(M_MIX0, 4, ones, acc[:, :])
        pe.wait_ge(rs_step, M_MIX0 + 1)
        e_load(E_KV, 0, 2, plain(256, 2), 4, 4)
        pe.wait_ge(gain_rows_loaded, 16 * GAIN_DMAS)
        pe.transpose(ps[:, 7, 0:N_GAINS], gain_rows[:, :], ident[0:N_GAINS, 0:N_GAINS]).then_inc(gains_turned, 1)
        e_load(E_KV + 1, 1, 2, plain(256, 2), 4, 4)
        pe.wait_ge(means_loaded, 16)
        pe.wait_ge(e_q_squared, 1)
        mean(M_EQ, 6, mean64, yb[:, 0, :])
        pe.wait_ge(gains_ready, 3)
        pe.wait_ge(e_q_squared, 2)
        mean(M_EQ + 1, 7, mean64, yb[:, 1, :])
        pe.wait_ge(e_q_scaled, 4)
        e_load(E_AIN, 0, 4, plain(512, 4), 0)
        pe.wait_ge(e_q_squared, 4)
        pe.wait_ge(rs_step, M_EQ + 1)
        mean(M_EQ + 2, 6, mean64, yb[:, 2, :])
        pe.wait_ge(rs_step, M_EQ + 2)
        mean(M_EQ + 3, 7, mean64, yb[:, 3, :])
        e_load(E_AIN + 1, 1, 4, plain(512, 4), 0)
        pe.wait_ge(e_k_squared, 1)
        pe.wait_ge(e_v_scaled, 1)
        mean(M_EK, 4, mean64, sq[:, 0, :])
        for t in range(QT):
            ins = pe.transpose(ps[:, 5, t * P:(t + 1) * P], e_vT[:, t * P:(t + 1) * P], ident)
        ins.then_inc(e_v_turned, 1)
        def e_scores(i):
            k0 = max(i - 1, 0)
            lo_ = 128 if i == 0 else 0
            if i:
                pe.wait_ge(a_biased, 4 * i)
            for h in (2, 6, 3, 7, 0, 4, 1, 5):
                if h == 0 and i >= 2:
                    pe.wait_ge(a_out, i - 1)
                a = 64 * (h // 4)
                c = 256 * (h % 2)
                ins = MM(ps[:, 4 + h // 2, c + lo_:c + 256], e_q[a:a + 64, h % 4, i * P:(i + 1) * P],
                         e_k[a:a + 64, k0 * P:(i + 1) * P], start=True, stop=True)
            ins.then_inc(a_scores, 1)

        def e_turn(i):
            pe.wait_ge(a_probs, HEADS * (i + 1))
            pe.wait_ge(a_biased, 4 * min(i + 2, QT))
            for kv in range(2):
                for part in ((1,) if i == 0 else (0, 1)):
                    for g in range(4):
                        ins = pe.transpose(ps[:, 4 + 2 * kv + part, g * P:(g + 1) * P],
                                           e_sc[:, i % 2, 4 * kv + g, part * P:(part + 1) * P], ident)
            ins.then_inc(a_probs_turned, 1)

        def e_values(i):
            if i:
                pe.wait_ge(a_pT_dve, 4 * i)
            else:
                pe.wait_ge(a_pT_act, 2)
            parts = (1,) if i == 0 else (0, 1)
            for part in parts:
                for kv in range(2):
                    ins = MM(ps[64 * kv:64 * kv + 64, 4, :], e_v[:, i - 1 + part, 64 * kv:64 * kv + 64],
                             e_pT[:, 2 * kv + part, :], start=part == parts[0], stop=part == 1)
            ins.then_inc(a_values, 1)

        ain = lambda j: e_load(E_AIN + j, j, 4, plain(512, 4), 0)
        ac = lambda j: e_load(E_AC + j, j, 4, plain(512, 4), 0)
        ab = lambda j, extra=None: e_load(E_AB + j, j, 4, plain(512, 4), 0, extra=extra)

        ain(2)
        pe.wait_ge(rs_used, 5)
        pe.wait_ge(e_v_ready, 1)
        e_scores(0)
        ain(3)
        e_scores(1)
        pe.wait_ge(conv_in_scaled, 4)
        ac(0)
        e_turn(0)
        ac(1)
        e_values(0)
        e_scores(2)
        ac(2)
        e_turn(1)
        ac(3)
        e_values(1)
        e_scores(3)
        pe.wait_ge(conv_h_ready, 4)
        ab(0)
        e_turn(2)
        ab(1, lambda: e_values(2))
        pe.wait_ge(a_out, 3)
        e_turn(3)
        ab(2, lambda: e_values(3))
        pe.wait_ge(yb_summed, 4)
        mean(M_EB, 5, ones, acc[:, :])
        ab(3)

        def out_group(n, b0, first2, last2, ready_sems, extra=None):
            for j in range(4):
                th, tl = first2 if j < 2 else last2
                pe.wait_ge(ready_sems[j // 2], 2 * (j % 2) + 2)
                load(n + j, plain(512, 4), range(2 * (j % 2), 2 * (j % 2) + 2), lambda k: (th[:, k, :], tl[:, k, :]),
                     range(b0, b0 + 4), j == 0, j == 3, extra=extra and (lambda: extra(j, 0)))
                if extra:
                    extra(j, 1)

        def ea_mean(j, part):
            if (j, part) != (0, 1):
                return
            pe.wait_ge(ya_ready, 4)
            pe.wait_ge(ya_summed, 4)
            mean(M_EA, 0, ones, acc[:, :])

        pe.wait_ge(rs_step, M_EB + 1)
        out_group(E_OUT, 4, (yb_hi, yb_lo), (ya_hi, ya_lo), (yb_lo_ready, ya_lo_ready), ea_mean)
        pe.wait_ge(rs_step, M_EA + 1)
        out_group(E_OUT + 4, 0, (yb_hi, yb_lo), (ya_hi, ya_lo), (yb_lo_ready, ya_lo_ready))

        def ffn_in(layer, bank0):
            n0, n1, c = FFN_IN[layer], FFN_OUT[layer], 22 * layer
            rnd = 1 + 2 * layer

            def half_group(n, j, b0, shift):
                load(n + j, plain(256, 2), range(4 * (j // 2), 4 * (j // 2) + 4), H,
                     (b0 + 2 * (j % 2), b0 + 2 * (j % 2) + 1), j < 2, j >= 2, shift)

            pe.wait_ge(x_ready, 8 * rnd + 4)
            for j in range(4):
                if j in (0, 2):
                    pe.wait_ge(h_lo_ready, 8 * rnd + 2 * j + 4)
                half_group(n0, j, 4 * bank0, 0)
                if j == 1:
                    pe.wait_ge(x_ready, 8 * rnd + 8)
                    pe.wait_ge(h_summed, 8 * rnd + 8)
                    mean(M_FFN0 if layer == 0 else M_FFN1, (1 - bank0) * 4, ones, acc[:, :])
            pe.wait_ge(rs_step, (M_FFN0 if layer == 0 else M_FFN1) + 1)
            with pe.Fori(0, NG_FF // 2) as i:
                for g in (1, 2):
                    pe.wait_ge(hidden_ready, 1 + c + 2 * (g - 1) + 4 * i)
                    for j in range(4):
                        half_group(n0 + 4 * g, j, 4 * ((bank0 + g) % 2), 8 * i)

        def ffn_out(layer, bank0, half, extra=None):
            c = 22 * layer
            b0 = 4 * ((bank0 + 11 + half) % 2)
            m = FFN_OUT[layer] + 11 * half
            banks = range(b0, b0 + 4)
            A = lambda k: (act_hi[:, k, :], act_lo[:, k, :])
            pe.wait_ge(hidden_ready, 1 + c + 20 + 2 * half)
            pe.wait_ge(hidden_lo, c + 20)
            load(m, plain(512, 4), (0, 1), A, banks, True, False)
            if extra:
                extra()
            with pe.Fori(0, 2) as i:
                for j in range(1, 5):
                    ready(m + j, 4 * i)
                    wh, wl = w_hi[:, (m + j) % W_SLOTS, :], w_lo[:, (m + j) % W_SLOTS, :]
                    for kk in range(2):
                        k = bass.ds(8 * i + 2 * j + kk, 1)
                        mh = act_hi[:, k, :].rearrange("p k n -> p (k n)")
                        ml = act_lo[:, k, :].rearrange("p k n -> p (k n)")
                        for t in range(4):
                            st = slice(512 * kk + P * t, 512 * kk + P * t + P)
                            ins = product(ps[:, b0 + t, :], wh[:, st], wl[:, st], mh, ml, False, False)
                    ins.then_inc(load_used, 1)
            for j in (9, 10):
                if j == 10:
                    pe.wait_ge(hidden_lo, c + 22)
                load(m + j, plain(512, 4), (2 * j, 2 * j + 1), A, banks, False, j == 10)

        ffn_in(0, 1)
        ffn_out(0, 1, 0)
        ffn_out(0, 1, 1)

        pe.wait_ge(x_ready, 20)
        for j in range(4):
            pe.wait_ge(h_lo_ready, 16 + 2 * j + 2)
            load(O_CQ + j, plain(384, 3), (2 * j, 2 * j + 1), H, range(3), j == 0, j == 3)
            if j == 2:
                pe.wait_ge(x_ready, 24)
                pe.wait_ge(h_summed, 24)
                mean(M_MIX1, 4, ones, acc[:, :])
                for t in range(QT):
                    ins = MM(ps[:, 5, t:t + 1], acc[:, t * P:(t + 1) * P], ones[:, 0:1], start=True, stop=True)
                ins.then_inc(tok_sums, 1)
        pe.wait_ge(rs_step, M_MIX1 + 1)
        pe.wait_ge(tok_step, 1)
        def cq_mean():
            pe.wait_ge(cq_summed, 3)
            mean(M_CQ, 3, ones, acc[:, :])

        for j in range(4):
            load(O_CKV + j, plain(384, 3), (2 * j, 2 * j + 1), H, range(4, 7), j == 0, j == 3,
                 extra=cq_mean if j == 1 else None)
        pe.wait_ge(rs_step, M_CQ + 1)
        pe.wait_ge(cq_scaled, 3)
        for j in range(4):
            n = O_CV + j
            ready(n)
            for kk in range(2):
                if (j, kk) == (1, 1):
                    pe.wait_ge(ckv_scaled, 3)
                    pe.wait_ge(ckv_summed, 2)
                    mean(M_CKV, 4, ones, acc[:, :])
                    pe.wait_ge(ckv_squared, 3)
                    mean(M_KR, 5, ones, sq[:, 0, :])
                if (j, kk) == (3, 1):
                    pe.wait_ge(kr_terms, 1)
                    MM(ps[:, 5, :], turn, kr[:, 0, :], start=True, stop=True).then_inc(kr_added, 1)
                c = slice(512 * kk, 512 * kk + 512)
                for t in range(QT):
                    ins = product(ps[:, t, :], h_hi[:, 2 * j + kk, t * P:(t + 1) * P], h_lo[:, 2 * j + kk, t * P:(t + 1) * P],
                                  w_hi[:, n % W_SLOTS, c], w_lo[:, n % W_SLOTS, c], j == 0 and kk == 0, j == 3 and kk == 1)
            ins.then_inc(load_used, 1)
            if j == 1:
                pe.wait_ge(spatial_loaded, 32)
                for b in range(2):
                    for g in range(4):
                        ins = pe.transpose(ps[:, 6 + b, g * P:(g + 1) * P], w_sp[:, 4 * b + g, :], ident)
                    ins.then_inc(spatial_turned, 1)

        def q_load(j, b0):
            tiles = lambda w, kk: [w[:, 256 * kk + P * t:256 * kk + P * t + P] for t in range(2)]
            load(O_UQ[j], tiles, range(3), lambda k: (cq_hi[:, k, :], cq_lo[:, k, :]), (b0, b0 + 1), True, True)

        def q_means(j, b0):
            for i in range(2):
                h = 2 * j + i
                pe.wait_ge(oq_turned, h + 1)
                mean(M_OQ + h, b0 + i, mean_odd if h % 2 else mean_even, q_sq(h))

        def cu_load(j, extra=None):
            load(O_CU[j], plain(512, 4), (2 * j, 2 * j + 1), H, range(4), j == 0, j == 3, extra=extra)

        pe.wait_ge(cq_lo_ready, 3)
        pe.wait_ge(rs_step, M_KR + 1)
        pe.wait_ge(spatial_ready, 2)
        pe.wait_ge(kr_rotated, 1)
        q_load(0, 4)
        q_load(1, 6)
        pe.wait_ge(cv_ready, 4)
        cu_load(0, lambda: q_means(0, 4))
        q_means(1, 6)
        cu_load(1)
        pe.wait_ge(rs_step, M_OQ + 2)
        q_load(2, 4)
        pe.wait_ge(rs_step, M_OQ + 4)
        q_load(3, 6)
        cu_load(2, lambda: q_means(2, 4))
        q_means(3, 6)
        cu_load(3)

        def kv_load(half):
            n = O_UKV + half
            ready(n)
            keys = lambda w, kk, j: w[:, n % W_SLOTS, 512 * kk + P * j:512 * kk + P * j + P]
            values = lambda w, kk: w[:, n % W_SLOTS, 512 * kk + 256:512 * kk + 512]

            def key_tiles():
                if half == 0:
                    pe.wait_ge(rs_step, M_OQ + 6)
                else:
                    pe.wait_ge(rs_step, M_OK + 2)
                for kk in range(2):
                    for j in range(2):
                        ins = product(ps[:, 4 + j, :], keys(w_hi, kk, j), keys(w_lo, kk, j),
                                      ckv_hi[:, kk, :], ckv_lo[:, kk, :], kk == 0, kk == 1)
                return ins

            def value_tiles():
                if half == 0:
                    pe.wait_ge(rs_step, M_OQ + 8)
                else:
                    pe.wait_ge(ov_act, 1)
                    pe.wait_ge(ov_dve, 1)
                for t in range(QT):
                    for kk in range(2):
                        c = 256 * (t % 2)
                        ins = product(ps[:, 6 + t // 2, c:c + 256], ckv_hi[:, kk, t * P:(t + 1) * P],
                                      ckv_lo[:, kk, t * P:(t + 1) * P], values(w_hi, kk), values(w_lo, kk),
                                      kk == 0, kk == 1)
                return ins

            if half == 0:
                key_tiles()
                ins = value_tiles()
            else:
                value_tiles()
                ins = key_tiles()
            ins.then_inc(load_used, 1)

        def k_means(half):
            for j in range(2):
                p = 2 * half + j
                pe.wait_ge(ok_gained, p + 1)
                mean(M_OK + p, K_MEAN_BANKS[p], mean64, sq[:, j, :])

        pe.wait_ge(ckv_lo_ready, 2)
        kv_load(0)
        pe.wait_ge(u_scaled, 4)
        pe.wait_ge(cv_normed, 4)
        for g0 in range(0, 8, 2):
            for t, g in ((t, g) for t in range(QT) for g in (g0, g0 + 1)):
                a = 64 * (g % 2)
                ins = MM(ps[a:a + 64, g // 2, t * P:(t + 1) * P], v_c[:, t, 64 * g:64 * g + 64], w_spT[:, g, :],
                         start=True, stop=True)
        ins.then_inc(gates_mixed, 1)
        k_means(0)
        kv_load(1)

        def o_scores(h):
            for n, i in enumerate(SCORE_ORDER):
                if h:
                    pe.wait_ge(d_exp_done, QT * (h - 1) + (1, 3, 3, 4)[n])
                s_ = score(i)
                MM(s_, o_q[:, h, i * P:(i + 1) * P], o_k[:, h, 0:P * (i + 1)], start=True, stop=False)
                MM(s_[:, P * i:P * (i + 1)], mask_q[:, :], mask_k[:, :], start=False, stop=True
                   ).then_inc(d_scores, 1)

        def o_turn(h):
            pe.wait_ge(d_probs, QT * (h + 1))
            if h:
                pe.wait_ge(d_pT_act, 2 * h)
                pe.wait_ge(d_pT_dve, h)
            for kt in range(QT):
                bank, c0 = ((4, 0), (5, 0), (6, 0), (5, 384))[kt]
                for i in range(kt, QT):
                    c = c0 + P * (i - kt)
                    ins = pe.transpose(ps[:, bank, c:c + P], o_p[:, h % 2, p_cols(i)][:, kt * P:(kt + 1) * P], ident)
            ins.then_inc(d_probs_turned, 1)

        def o_values(h):
            a = 64 * (h % 2)
            pe.wait_ge(d_pT_act, 2 * (h + 1))
            pe.wait_ge(d_pT_dve, h + 1)
            if h:
                pe.wait_ge(d_out, h)
            for kt in range(QT):
                pT = (o_pT[:, 0, :], o_pT[:, 1, 0:384], o_pT[:, 2, 0:256], o_pT[:, 1, 384:512])[kt]
                ins = MM(ps[a:a + 64, 7, P * kt:S], o_v[:, kt, 64 * h:64 * h + 64], pT,
                         start=kt == 0, stop=kt == QT - 1)
            ins.then_inc(d_values, 1)

        pe.wait_ge(gates_ready, 4)
        pe.wait_ge(kr_copied, HEADS)
        pe.wait_ge(columns_set, 1)
        pe.wait_ge(rs_used, used_before(M_OK + 1))
        o_scores(0)
        pe.wait_ge(ov_dve, 2)
        k_means(1)
        o_scores(1)
        pe.wait_ge(ov_act, 2)
        for h in range(HEADS):
            if h == 3:
                pe.wait_ge(rs_used, used_before(M_OK + 3))
                pe.wait_ge(ok_normed, 4)
            if 0 < h < HEADS - 1:
                o_scores(h + 1)
            if h == 1:
                pe.wait_ge(rs_step, M_OK + 4)
            if h:
                o_values(h - 1)
            o_turn(h)
            if h == 1:
                pe.wait_ge(yc_summed, 4)
                mean(M_OC, 3, ones, acc[:, :])

        def od_mean(j, part):
            if (j, part) == (0, 0):
                o_values(7)
            if (j, part) == (0, 1):
                pe.wait_ge(yd_summed, 4)
                mean(M_OD, 4, ones, acc[:, :])

        pe.wait_ge(rs_step, M_OC + 1)
        out_group(O_OUT, 0, (yc_hi, yc_lo), (yd_hi, yd_lo), (yc_lo_ready, yd_lo_ready), od_mean)
        pe.wait_ge(rs_step, M_OD + 1)
        out_group(O_OUT + 4, 4, (yc_hi, yc_lo), (yd_hi, yd_lo), (yc_lo_ready, yd_lo_ready))
        ffn_in(1, 0)

        def turn_out(half):
            if half:
                pe.wait_ge(out_act, 2)
                pe.wait_ge(out_dve, 2)
            else:
                pe.wait_ge(x_ready, 32 + 4)
            for j in range(4):
                pe.wait_ge(x_ready, 32 + 4 * half + j + 1)
                for t in range(QT):
                    ins = pe.transpose(ps[:, 4 + t, j * P:(j + 1) * P], xT[:, 4 * half + j, t * P:(t + 1) * P], ident)
                    if j == 3:
                        ins.then_inc(out_turned, 1)

        ffn_out(1, 0, 0)
        ffn_out(1, 0, 1, lambda: turn_out(0))
        turn_out(1)
    ctx.close()


_INS = ["x", "mix_norm", "ffn_norm", "w_ffn_in", "w_ffn_out", "e_w_in", "e_conv", "e_q_gain", "e_k_gain",
        "e_sinks", "e_out_gain", "e_w_out", "o_w_in", "o_spatial", "o_spatial_bias", "o_v_gain",
        "o_q_a_gain", "o_kv_a_gain", "o_w_uq", "o_w_ukv", "o_q_gain", "o_k_gain", "o_out_gain", "o_w_out"]


def constants():
    f = np.float32
    blk = np.zeros((3, P, P), f)
    for a in (0, 64):
        blk[0, a:a + 64, a:a + 64] = 1 / 64
    blk[1, 0:64, 0:64] = 1 / 64
    blk[1, 64:96, 64:128] = 1 / 32
    blk[2, 64:128, 64:128] = 1 / 64
    blk[2, 0:32, 0:64] = 1 / 32
    turn = np.zeros((P, P), f)
    for p in range(P):
        turn[p % 32, p] = turn[32 + p % 32, p] = 1
    small = np.concatenate([np.eye(P, dtype=f), np.ones((P, P), f), blk[0], blk[1], blk[2], turn], axis=1)
    pos = np.arange(S, dtype=f)
    inv = (f(10000.0) ** (-np.arange(0, 32, 2, dtype=f) / f(32))).astype(f)
    ang = (pos[None, :] * inv[:, None]).astype(f)
    cos = np.concatenate([np.cos(ang)] * 2)
    sin = np.concatenate([-np.sin(ang), np.sin(ang)])
    one = np.ones((64, S), f)
    tables = np.concatenate([np.tile(np.concatenate([cos, sin]), (2, 1)),
                             np.concatenate([one, cos, sin]), np.concatenate([cos, sin, one])], axis=1)
    q, k = np.arange(P)[:, None], np.arange(256)[None, :] - P
    seen = (k // 64 <= q // 64) & (k // 64 >= q // 64 - 1)
    slopes = 2.0 ** -np.arange(1, HEADS + 1)
    alibi = np.where(seen[:, None, :], -slopes[None, :, None] * np.abs(q - k)[:, None, :], NEG)
    return small.astype(f), tables.astype(f), alibi.reshape(P, HEADS * 256).astype(f)


def kernel(**inputs):
    import concourse.bacc as bacc
    from concourse.bass_utils import run_bass_kernel_spmd as run

    nc = bacc.Bacc("TRN2", target_bir_lowering=False, num_devices=1)
    arrays, args = {}, []
    for name in _INS:
        a = np.ascontiguousarray(inputs[name])
        arrays[f"in_{name}"] = a
        args.append(nc.dram_tensor(f"in_{name}", a.shape, mybir.dt.from_np(a.dtype), kind="ExternalInput").ap())
    for name, a in zip(("small", "tables", "alibi"), constants()):
        a = np.ascontiguousarray(a)
        arrays[f"const_{name}"] = a
        args.append(nc.dram_tensor(f"const_{name}", a.shape, F32, kind="ExternalInput").ap())
    args.append(nc.dram_tensor("out_0_dram", (1, S, D), F32, kind="ExternalOutput").ap())
    program(nc, *args)
    r = run(nc, [arrays], core_ids=[0])
    return r.results[0]["out_0_dram"]
```
